# Optimizing a Trainium2 kernel written in Bass

```python
import jax, jax.numpy as jnp
from jax import lax
import numpy as np

D_MODEL = 2048
BATCH = 1
SEQ = 256
DEPTH = 1
DEC_BATCH = 8
DEC_SEQ = 4
PAST_LEN = 2048
PAGE_SIZE = 128

D_CONF = D_MODEL
CONF_WIDTH = 31
D_SC = D_MODEL
SC_WIDTH = 3
N_PEER_HEADS = 8
N_KEYS = 128
N_EXPERTS = N_KEYS * N_KEYS
TOPK = 16
D_QUERY = D_MODEL // N_PEER_HEADS
D_SUBKEY = D_QUERY // 2
PEER_BLOCK = 128
ALPHA = (2.0 * DEPTH) ** 0.25
BETA = (8.0 * DEPTH) ** -0.25
LN_EPS = 1e-5
N_IN_COLS = 2 * D_CONF + 3 * D_SC + 2 * D_MODEL
IN_SPLITS = (D_CONF, 2 * D_CONF, 2 * D_CONF + D_SC, 2 * D_CONF + 2 * D_SC,
             2 * D_CONF + 3 * D_SC, 2 * D_CONF + 3 * D_SC + D_MODEL)

kernel_name = 'conformer_shortconv_peer_hybrid_step'

def _layernorm(x, g, b):
    xf = x.astype(jnp.float32)
    mu = jnp.mean(xf, -1, keepdims=True)
    var = jnp.mean(jnp.square(xf - mu), -1, keepdims=True)
    y = (xf - mu) * lax.rsqrt(var + LN_EPS) * g.astype(jnp.float32) + b.astype(jnp.float32)
    return y.astype(x.dtype)

def _causal_dwconv(buf, x, w):
    xp = jnp.concatenate([buf, x], axis=1)
    y = lax.conv_general_dilated(xp, w[:, None, :], window_strides=(1,), padding='VALID',
                                 dimension_numbers=('NWC', 'WIO', 'NWC'),
                                 feature_group_count=x.shape[-1])
    return y, xp[:, -(w.shape[0] - 1):]

def _peer(u, w_q, sub_keys, peer_u, peer_v):
    T = u.shape[0]
    n_blk = -(-T // PEER_BLOCK)
    up = jnp.pad(u, ((0, n_blk * PEER_BLOCK - T), (0, 0))).reshape(n_blk, PEER_BLOCK, D_MODEL)

    def block(ub):
        q = (ub @ w_q).reshape(PEER_BLOCK, N_PEER_HEADS, 2, D_SUBKEY)
        s = jnp.einsum('thpk,hpnk->thpn', q, sub_keys).astype(jnp.float32)
        v, i = lax.top_k(s, TOPK)
        cand = (v[:, :, 0, :, None] + v[:, :, 1, None, :]).reshape(PEER_BLOCK, N_PEER_HEADS, TOPK * TOPK)
        sc, pos = lax.top_k(cand, TOPK)
        i1 = jnp.take_along_axis(i[:, :, 0], pos // TOPK, axis=-1)
        i2 = jnp.take_along_axis(i[:, :, 1], pos % TOPK, axis=-1)
        eid = (i1 * N_KEYS + i2).reshape(PEER_BLOCK, N_PEER_HEADS * TOPK)
        g = jax.nn.softmax(sc, axis=-1).reshape(PEER_BLOCK, N_PEER_HEADS * TOPK).astype(ub.dtype)
        act = jax.nn.gelu(jnp.einsum('td,tkd->tk', ub, peer_u[eid]), approximate=False)
        return jnp.einsum('tk,tkd->td', g * act, peer_v[eid])

    out = lax.map(block, up)
    return out.reshape(n_blk * PEER_BLOCK, D_MODEL)[:T]

def _layer(x, c, buf_a, buf_b, w_mod, b_mod, w_in, conv_a_w, conv_a_b, ln_a_g, ln_a_b, w_a_out,
           conv_b_w, w_b_out, w_o, ln1_g, ln1_b, w_q, sub_keys, peer_u, peer_v, ln2_g, ln2_b):
    N, L, _ = x.shape
    mod = jax.nn.silu(c) @ w_mod + b_mod
    sh1, sc1, g1, sh2, sc2, g2 = jnp.split(mod[:, None, :], 6, axis=-1)

    u = x * (1 + sc1) + sh1
    z = u @ w_in
    a_val, a_gate, b_gate, c_gate, h, gate_a, gate_b = jnp.split(z, IN_SPLITS, axis=-1)
    glu = a_val * jax.nn.sigmoid(a_gate)
    ya, new_a = _causal_dwconv(buf_a, glu, conv_a_w)
    ya = jax.nn.silu(_layernorm(ya + conv_a_b, ln_a_g, ln_a_b)) @ w_a_out
    yb, new_b = _causal_dwconv(buf_b, c_gate * h, conv_b_w)
    yb = (b_gate * yb) @ w_b_out
    m = (jax.nn.sigmoid(gate_a) * ya + jax.nn.sigmoid(gate_b) * yb) @ w_o
    x = _layernorm(ALPHA * x + (1 + g1) * m, ln1_g, ln1_b)

    u2 = x * (1 + sc2) + sh2
    f = _peer(u2.reshape(N * L, D_MODEL), w_q, sub_keys, peer_u, peer_v).reshape(N, L, D_MODEL)
    x = _layernorm(ALPHA * x + (1 + g2) * f, ln2_g, ln2_b)
    return x, new_a, new_b

def setup_inputs(seed: int = 0) -> dict:
    key = jax.random.key(seed)
    ks = jax.random.split(key, 25)
    D = D_MODEL
    L = DEPTH

    def nrm(k, shape, s):
        return jax.random.normal(k, shape, jnp.float32) * s

    return {
        'x_prompt': nrm(ks[0], (BATCH, SEQ, D), 1.0),
        'x_sample': nrm(ks[1], (DEC_BATCH, DEC_SEQ, D), 1.0),
        'state_conv_a': nrm(ks[2], (L, DEC_BATCH, CONF_WIDTH - 1, D_CONF), 0.5),
        'state_conv_b': nrm(ks[3], (L, DEC_BATCH, SC_WIDTH - 1, D_SC), 0.5),
        'c_prompt': nrm(ks[4], (BATCH, D), 1.0),
        'c_sample': nrm(ks[5], (DEC_BATCH, D), 1.0),
        'w_mod': nrm(ks[6], (L, D, 6 * D), 0.1 * D ** -0.5),
        'b_mod': nrm(ks[7], (L, 6 * D), 0.01),
        'w_in': nrm(ks[8], (L, D, N_IN_COLS), D ** -0.5),
        'conv_a_w': nrm(ks[9], (L, CONF_WIDTH, D_CONF), CONF_WIDTH ** -0.5),
        'conv_a_b': nrm(ks[10], (L, D_CONF), 0.01),
        'ln_a_g': 1.0 + nrm(ks[11], (L, D_CONF), 0.02),
        'ln_a_b': nrm(ks[12], (L, D_CONF), 0.02),
        'w_a_out': nrm(ks[13], (L, D_CONF, D), D_CONF ** -0.5),
        'conv_b_w': nrm(ks[14], (L, SC_WIDTH, D_SC), SC_WIDTH ** -0.5),
        'w_b_out': nrm(ks[15], (L, D_SC, D), D_SC ** -0.5),
        'w_o': nrm(ks[16], (L, D, D), BETA * D ** -0.5),
        'ln1_g': 1.0 + nrm(ks[17], (L, D), 0.02),
        'ln1_b': nrm(ks[18], (L, D), 0.02),
        'w_q': nrm(ks[19], (L, D, N_PEER_HEADS * D_QUERY), D ** -0.5),
        'sub_keys': nrm(ks[20], (L, N_PEER_HEADS, 2, N_KEYS, D_SUBKEY), D_SUBKEY ** -0.5),
        'peer_u': nrm(ks[21], (L, N_EXPERTS, D), D ** -0.5),
        'peer_v': nrm(ks[22], (L, N_EXPERTS, D), BETA),
        'ln2_g': 1.0 + nrm(ks[23], (L, D), 0.02),
        'ln2_b': nrm(ks[24], (L, D), 0.02),
    }

def reference(x_prompt, x_sample, state_conv_a, state_conv_b, c_prompt, c_sample,
              w_mod, b_mod, w_in, conv_a_w, conv_a_b, ln_a_g, ln_a_b, w_a_out,
              conv_b_w, w_b_out, w_o, ln1_g, ln1_b, w_q, sub_keys, peer_u, peer_v,
              ln2_g, ln2_b):
    layer_w = (w_mod, b_mod, w_in, conv_a_w, conv_a_b, ln_a_g, ln_a_b, w_a_out,
               conv_b_w, w_b_out, w_o, ln1_g, ln1_b, w_q, sub_keys, peer_u, peer_v,
               ln2_g, ln2_b)
    nb = x_prompt.shape[0]
    zero_a = jnp.zeros((nb, CONF_WIDTH - 1, D_CONF), x_prompt.dtype)
    zero_b = jnp.zeros((nb, SC_WIDTH - 1, D_SC), x_prompt.dtype)
    yp, ys = x_prompt, x_sample
    na_p, nb_p, na_s, nb_s = [], [], [], []
    for l in range(DEPTH):
        wl = [w[l] for w in layer_w]
        yp, a_p, b_p = _layer(yp, c_prompt, zero_a, zero_b, *wl)
        ys, a_s, b_s = _layer(ys, c_sample, state_conv_a[l], state_conv_b[l], *wl)
        na_p.append(a_p)
        nb_p.append(b_p)
        na_s.append(a_s)
        nb_s.append(b_s)
    new_conv_a_prompt = jnp.stack(na_p)
    new_conv_b_prompt = jnp.stack(nb_p)
    new_conv_a_sample = jnp.stack(na_s)
    new_conv_b_sample = jnp.stack(nb_s)
    return (yp, ys, new_conv_a_prompt, new_conv_b_prompt, new_conv_a_sample, new_conv_b_sample)


_drawn_inputs = setup_inputs


def setup_inputs(seed=0):
    import zlib

    import numpy as np

    out = dict(_drawn_inputs(seed))
    spreads = {}
    factors = {'conv_a_b': 3.774, 'ln_a_g': 3.44, 'ln_a_b': 3.709, 'ln2_g': 2.885, 'ln2_b': 2.837}
    for name, (base, spread) in spreads.items():
        noise = np.random.default_rng([zlib.crc32(name.encode()), seed]).standard_normal(out[name].shape)
        drawn = base * np.exp(spread * noise) if base else spread * noise
        out[name] = __import__('jax').numpy.asarray(drawn.astype(out[name].dtype))
    for name, factor in factors.items():
        out[name] = (out[name] * factor).astype(out[name].dtype)
    return out
```

```python
from contextlib import ExitStack

import concourse.bass as bass
from concourse import mybir

F32 = mybir.dt.float32
F32R = mybir.dt.float32r
U32 = mybir.dt.uint32
ALU = mybir.AluOpType
ACT = mybir.ActivationFunctionType
AX = mybir.AxisListType

P = 128
D = 2048
NCH = D // P
SEQ, DEC_B, DEC_T = 256, 8, 4
TS = DEC_B * DEC_T
N = SEQ + TS
WA, WB = 31, 3
HA, HB = WA - 1, WB - 1
HEADS, NKEYS, TOPK = 8, 128, 16
ALPHA = 2.0 ** 0.25
EPS = 1e-5

GC = 4
NG = NCH // GC
UNITS = 8
RING = 4
NMOD = 6 * NG
PRE = 10
NQ = 7
A_GATE, A_VAL, C_GATE, H_IN, B_GATE, GATE_A, GATE_B = 1, 0, 3, 4, 2, 5, 6
ORDER = [A_GATE, A_VAL, C_GATE, H_IN, B_GATE, GATE_A, GATE_B]
NIN = NQ * NG
PER = UNITS + GC
SH1, SC1, G1, SH2, SC2, G2 = range(6)

R_WA, R_WB, R_BA, R_AG, R_AB, R_1G, R_1B, R_MOD, R_C = 0, 31, 34, 35, 36, 37, 38, 39, 45
NROW = 45 + 1 + DEC_B
NMC = 1 + DEC_B

BLOCKS = [(0, 1, 16), (1, 1, 8), (2, 2, 5), (4, 4, 3), (8, 8, 1)]
NCAND = sum(r * n for _, r, n in BLOCKS)
LOWEST = -3.4e38

TILES = [(0, 1), (2, 9), (10, 17)]
STEPS = 18
ROWS = [TS, P, P]


MOD_AT = (2, 4, 7, 10)


def main_of(j):
    return None if j in MOD_AT else j - sum(m < j for m in MOD_AT)


def at_least(eng, sem, value):
    if isinstance(value, int):
        if value > 0:
            eng.wait_ge(sem, value)
    else:
        eng.wait_ge(sem, value)


def at_least_apart(eng, sem, value):
    at_least(eng, sem, value)
    if not isinstance(value, int):
        eng.nop(nofuse=True)


class Chain:

    def __init__(self, eng, sem):
        self.eng, self.sem, self.n = eng, sem, 0

    def restart(self):
        self.all()
        self.eng.sem_clear(self.sem)
        self.n = 0

    def link(self, ins):
        ins.then_inc(self.sem, 1)
        self.n += 1
        return self

    def all(self):
        at_least(self.eng, self.sem, self.n)

    def back(self, k):
        at_least(self.eng, self.sem, self.n - k)


def hybrid_step(nc, x_prompt, x_sample, state_a, state_b, c_prompt, c_sample, w_mod, b_mod, w_in,
                conv_a_w, conv_a_b, ln_a_g, ln_a_b, w_a_out, conv_b_w, w_b_out, w_o, ln1_g, ln1_b,
                w_q, sub_keys, peer_u, peer_v, ln2_g, ln2_b,
                y_prompt, y_sample, new_a_prompt, new_b_prompt, new_a_sample, new_b_sample):
    with ExitStack() as ctx:
        base = 16512

        def at(name, offset, shape, dt=F32):
            return nc.alloc_sbuf_tensor_at(name, shape, dt, offset=base + offset)

        def sem(name):
            return ctx.enter_context(nc.semaphore(name))

        R = NCH * N * 4
        xT = at("xT", 0, [P, NCH, N])
        ybT = at("ybT", R, [P, NCH, N])
        actH = at("actH", 2 * R, [P, NCH, N], F32R)
        actL = at("actL", 3 * R, [P, NCH, N], F32R)
        cyT = at("cyT", 4 * R, [P, NCH, N])
        wH = at("wH", 5 * R, [P, RING, 2, 512], F32R)
        wL = at("wL", 5 * R + 16384, [P, RING, 2, 512], F32R)
        sgB = at("sgB", 124928, [P, NCH, N])
        raw = at("raw", 143360, [P, RING, 2, 512])
        sgA = at("sgA", 159744, [P, NCH, N])
        M0 = 178176
        gluP = at("gluP", M0, [P, GC, HA + SEQ])
        gluS = at("gluS", M0 + 4576, [P, GC, DEC_B, HA + DEC_T])
        cbP = at("cbP", M0 + 8928, [P, GC, HB + SEQ])
        cbS = at("cbS", M0 + 13056, [P, GC, DEC_B, HB + DEC_T])
        tmp = at("tmp", M0 + 13824, [P, GC, N])
        acc = at("acc", M0 + 18432, [P, GC, N])
        modT = at("modT", M0 + 23040, [P, 6 * NCH, NMC])
        par = at("par", M0 + 26496, [P, NCH, NROW])
        ident = at("ident", M0 + 29952, [P, P])
        ones = at("ones", M0 + 30464, [P, P])
        siluC = at("siluC", M0 + 30976, [P, NCH, NMC])
        mean = at("mean", M0 + 31552, [P, N])
        rstd = at("rstd", M0 + 32704, [P, N])
        tail = at("tail", M0 + 31552, [P, GC, 96])
        wAg = at("wAg", M0 + 33856, [P, GC, WA])
        wBg = at("wBg", M0 + 34368, [P, GC, WB + 1])
        zero = at("zero", M0 + 34432, [P, GC * NMC])
        xRaw = at("xRaw", 159744, [P, 2, D])
        parRaw = at("parRaw", 124928, [NROW, D])
        xsRaw = at("xsRaw", 124928 + 8192, [TS, D])
        stARaw = at("stARaw", R, [4 * HA, 2, D])
        stBRaw = at("stBRaw", 2 * R, [DEC_B * HB, D])
        tails = at("tails", M0 + 13824, [P, NCH, 96])
        keyRaw = at("keyRaw", 124928, [P, 2 * HEADS, P])
        sampleM = at("sampleM", M0 + 8192, [P, GC, DEC_B, DEC_T])
        keyT = at("keyT", M0, [P, 2 * HEADS, P])
        outA = at("outA", 124928 + 8192, [HA + TS, D])
        outB = at("outB", 159744, [HB + TS, D])
        fin = at("fin", 0, [P, D])
        g2S = at("g2S", 8192, [TS, D])
        uRing = at("uRing", 2 * R, [P, 4, D])
        vRing = at("vRing", 2 * R + 32768, [P, 4, D])
        u2Rep = at("u2Rep", 92160, [P, NCH, P])
        g2sRep = at("g2sRep", 100352, [P, NCH, TS])
        g2pRep = at("g2pRep", 102400, [P, NCH, P])
        diag = at("diag", 102400, [P, TOPK, P])
        x1Tok = at("x1Tok", 110592, [P, 3, D])
        lnG = at("lnG", 135168, [P, D])
        lnB = at("lnB", 143360, [P, D])
        g2P = at("g2P", 151552, [P, D])
        scores = at("scores", 159744, [P, STEPS, 2, NKEYS])
        T0 = M0 + 13824
        sc0 = at("sc0", T0, [P, 2, NKEYS])
        sc1 = at("sc1", T0 + 1024, [P, 2, NKEYS])
        onehot = at("onehot", T0 + 2048, [P, TOPK, NCAND])
        iota = at("iota", T0 + 5504, [P, NCAND], mybir.dt.int32)
        iotaF = at("iotaF", T0 + 5728, [P, NCAND])
        cand = at("cand", T0 + 5952, [P, NCAND])
        cand2 = at("cand2", T0 + 6176, [P, NCAND])
        candId = at("candId", T0 + 6400, [P, NCAND])
        top = at("top", T0 + 6624, [P, 2, TOPK])
        topIx = at("topIx", T0 + 6752, [P, 2, TOPK], U32)
        topIxF = at("topIxF", T0 + 6880, [P, 2, TOPK])
        pos = at("pos", T0 + 7008, [P, TOPK], U32)
        posF = at("posF", T0 + 7072, [P, TOPK])
        best = at("best", T0 + 7136, [P, 2, TOPK])
        negMax = at("negMax", T0 + 7264, [P, 2])
        eidF = at("eidF", T0 + 7296, [P, TOPK])
        idxU = at("idxU", T0 + 7360, [P, 2, TOPK], U32)
        idxV = at("idxV", T0 + 7488, [P, 2, TOPK], U32)
        dots = at("dots", T0 + 7616, [P, 2, TOPK])
        gel = at("gel", T0 + 7744, [P, TOPK])
        ex = at("ex", T0 + 7808, [P, TOPK])
        exSum = at("exSum", T0 + 7872, [P, 1])
        exInv = at("exInv", T0 + 7904, [P, 1])
        wts = at("wts", T0 + 7936, [P, 2, TOPK])
        fold = at("fold", T0 + 8064, [P, TS])
        stats = at("stats", T0 + 8192, [P, 4, 6])
        mv = at("mv", T0 + 8288, [P, 2])
        ve = at("ve", T0 + 8320, [P, 3])

        ps = ctx.enter_context(nc.psum_tensor("ps", [P, 8, 512], F32))

        tailScratch = nc.dram_tensor("tail_scratch", (P, NCH * 96), F32, kind="Internal").ap()

        loaded_par = sem("loaded_par")
        loaded_x = sem("loaded_x")
        loaded_state = sem("loaded_state")
        const_ready = sem("const_ready")
        pool_chain = sem("pool_chain")
        turned = sem("turned")
        turned_out = sem("turned_out")
        mod_begun = sem("mod_begun")
        raw_in = [sem(f"raw_in{k}") for k in range(RING)]
        hi_ready = sem("hi_ready")
        lo_ready = sem("lo_ready")
        mm_unit = sem("mm_unit")
        mod_unit = sem("mod_unit")
        mod_out = sem("mod_out")
        psum_free = sem("psum_free")
        src_ready = sem("src_ready")
        act_hi = sem("act_hi")
        act_lo = sem("act_lo")
        conv_done = sem("conv_done")
        conv_kept = sem("conv_kept")
        tail_ready = sem("tail_ready")
        tail_saved = sem("tail_saved")
        tail_back = sem("tail_back")
        v_chain = sem("v_chain")
        a_chain = sem("a_chain")
        x_scaled = sem("x_scaled")
        sum_done = sem("sum_done")
        mean_ready = sem("mean_ready")
        centred = sem("centred")
        squared = sem("squared")
        sq_done = sem("sq_done")
        var_ready = sem("var_ready")
        sd_ready = sem("sd_ready")
        normed = sem("normed")
        affine = sem("affine")
        key_in = sem("key_in")
        side_turned = sem("side_turned")
        side_out = sem("side_out")
        new_out = sem("new_out")
        ln_in = sem("ln_in")
        gates_done = sem("gates_done")
        scored = sem("scored")
        scores_out = sem("scores_out")
        rep_ready = sem("rep_ready")
        u2_ready = sem("u2_ready")
        idx_ready = sem("idx_ready")
        idxv_ready = sem("idxv_ready")
        u_in = [sem(f"u_in{k}") for k in range(4)]
        v_in = [sem(f"v_in{k}") for k in range(4)]
        dot_done = sem("dot_done")
        act_done = sem("act_done")
        wts_ready = sem("wts_ready")
        diag_ready = sem("diag_ready")
        v_done = sem("v_done")
        f_free = sem("f_free")
        fs_ready = sem("fs_ready")
        folded = sem("folded")
        ve_ready = sem("ve_ready")
        sdev_ready = sem("sdev_ready")
        y_ready = sem("y_ready")
        y_out = sem("y_out")
        state_out = sem("state_out")

        w_in_v = w_in.rearrange("(k p) n -> p k n", p=P)
        w_mod_v = w_mod.rearrange("(k p) n -> p k n", p=P)
        tails_w = [w.rearrange("(k p) n -> p k n", p=P) for w in (w_b_out, w_a_out, w_o, w_q)]
        C_OUT = NIN
        MODS = PRE * UNITS
        block = ctx.enter_context(nc.Block())

        def bank_set(c):
            return 4 * (c % 2) if isinstance(c, int) else (c & 1) * 4

        def group(c, lo=0, hi=N):
            return ps[:, bass.ds(bank_set(c), 4), lo:hi]

        def mod_bank(c):
            b = 4 - bank_set(c)
            return ps[:, bass.ds(b, 1), N:N + GC * NMC].rearrange("p a (n r) -> p (a n) r", n=GC)

        def raw_count(c, j):
            return 16 * (MODS // RING + 3 * c + j // RING + 1)

        def raw_count_out(c, u):
            return 16 * (MODS // RING + 3 * NIN + 2 * (c - C_OUT) + u // RING + 1)

        @block.sync
        def _(sp):
            rows = [(conv_a_w, R_WA, WA), (conv_b_w, R_WB, WB), (conv_a_b, R_BA, 1), (ln_a_g, R_AG, 1),
                    (ln_a_b, R_AB, 1), (ln1_g, R_1G, 1), (ln1_b, R_1B, 1), (b_mod, R_MOD, 6),
                    (c_prompt, R_C, 1), (c_sample, R_C + 1, DEC_B)]
            for src, r, n in rows:
                sp.dma_start(parRaw[r:r + n, :], src).then_inc(loaded_par, 16)

            def mod_units(c):
                for u in range(UNITS):
                    at_least_apart(sp, mod_unit, UNITS * c + u - RING + 1)
                    sp.dma_start(raw[:, u % RING], w_mod_v[:, 2 * u:2 * u + 2, bass.ds(c * 512, 512)])\
                      .then_inc(raw_in[u % RING], 16)

            sp.dma_start(xRaw[:, :, :], x_prompt.rearrange("(t p) d -> p t d", p=P)).then_inc(loaded_x, 16)
            sp.dma_start(xsRaw[:, :], x_sample).then_inc(loaded_x, 16)
            mod_units(0)
            mod_units(1)
            sp.dma_start(stARaw[:, :, :], state_a.rearrange("(h q) d -> q h d", h=2)).then_inc(loaded_state, 16)
            sp.dma_start(stBRaw[:, :], state_b).then_inc(loaded_state, 16)
            with sp.Fori(2, PRE) as c:
                mod_units(c)

            def in_group(g, q):
                c = NQ * g + q
                col = ORDER[q] * D + g * 512
                for j in range(PER):
                    k, cb = (j - RING, c) if j >= RING else (j - RING + PER, c - 1)
                    if isinstance(cb, int) and cb < 0:
                        at_least_apart(sp, mod_unit, MODS - RING + j + 1)
                    elif main_of(k) is None:
                        at_least_apart(sp, mod_unit, MODS + GC * cb + MOD_AT.index(k) + 1)
                    else:
                        at_least_apart(sp, lo_ready, UNITS * cb + main_of(k) + 1)
                    u = main_of(j)
                    if u is None:
                        half = (c & 1) * (NCH // 2)
                        src = w_mod_v[:, bass.ds(half + 2 * MOD_AT.index(j), 2), bass.ds((PRE + (c // 2)) * 512, 512)]
                    else:
                        src = w_in_v[:, 2 * u:2 * u + 2, bass.ds(col, 512)]
                    sp.dma_start(raw[:, j % RING], src).then_inc(raw_in[j % RING], 16)

            for q in range(NQ):
                in_group(0, q)
            with sp.Fori(1, NG) as g:
                for q in range(NQ):
                    in_group(g, q)

            for w, src in enumerate(tails_w):
                def out_group(i, first):
                    c = C_OUT + NG * w + i
                    for u in range(UNITS):
                        if u >= RING:
                            at_least_apart(sp, lo_ready, UNITS * c + u - RING + 1)
                        elif first and w == 0:
                            j = PER - RING + u
                            if main_of(j) is None:
                                at_least_apart(sp, mod_unit, MODS + GC * NIN)
                            else:
                                at_least_apart(sp, lo_ready, UNITS * (NIN - 1) + main_of(j) + 1)
                        else:
                            at_least_apart(sp, lo_ready, UNITS * (c - 1) + u + RING + 1)
                        sp.dma_start(raw[:, u % RING], src[:, 2 * u:2 * u + 2, bass.ds(i * 512, 512)])\
                          .then_inc(raw_in[u % RING], 16)

                out_group(0, True)
                with sp.Fori(1, NG) as i:
                    out_group(i, False)
                if w == 2:
                    sp.wait_ge(gates_done, 1)
                    sp.dma_start(keyRaw[:, :, :], sub_keys.rearrange("h s n k -> n (h s) k"),
                                 ).then_inc(key_in, 16)
            at_least_apart(sp, lo_ready, UNITS * (C_OUT + 4 * NG))
            sp.wait_ge(side_out, 3)
            sp.wait_ge(new_out, 16 * (2 + 1 + DEC_B))
            sp.dma_start(lnG[:, :], ln2_g.broadcast_to((P, D))).then_inc(ln_in, 16)
            sp.dma_start(lnB[:, :], ln2_b.broadcast_to((P, D))).then_inc(ln_in, 16)
            for t in range(3):
                sp.wait_ge(y_ready, t + 1)
                dst = y_sample if t == 0 else y_prompt[(t - 1) * P:t * P, :]
                sp.dma_start(dst, fin[0:ROWS[t], :]).then_inc(y_out, 16)
            sp.wait_ge(y_out, 48)

        @block.gpsimd
        def _(pool):
            nc.gpsimd.memset(ident[:, :], 0.0).then_inc(pool_chain, 1)
            pool.wait_ge(pool_chain, 1)
            nc.gpsimd.affine_select(out=ident[:, :], in_=ident[:, :], compare_op=ALU.not_equal, fill=1.0,
                                    base=0, pattern=[[-1, P]], channel_multiplier=1).then_inc(const_ready, 1)
            nc.gpsimd.memset(ones[:, :], 1.0).then_inc(const_ready, 1)
            nc.gpsimd.memset(zero[:, :], 0.0).then_inc(const_ready, 1)
            nc.gpsimd.memset(gluP[:, :, 0:HA], 0.0).then_inc(const_ready, 1)
            nc.gpsimd.memset(cbP[:, :, 0:HB], 0.0).then_inc(const_ready, 1)
            pool.dma_start(new_a_sample[:, 0:HA - DEC_T, :],
                           state_a.rearrange("(b r) d -> b r d", r=HA)[:, DEC_T:HA, :]).then_inc(state_out, 16)
            with pool.Fori(0, NG) as g:
                at_least_apart(pool, tail_ready, g + 1)
                pool.dma_start(tailScratch[:, bass.ds(g * GC * 96, GC * 96)],
                               tail[:, :, :].rearrange("p a b -> p (a b)")).then_inc(tail_saved, 16)
            pool.wait_ge(tail_saved, 16 * NG)
            pool.wait_ge(psum_free, NIN)
            pool.wait_ge(conv_kept, NG)
            pool.dma_start(tails[:, :, :].rearrange("p a b -> p (a b)"), tailScratch).then_inc(tail_back, 16)
            pool.wait_ge(side_out, 3)
            pool.dma_start(new_a_prompt, outA[0:HA, :]).then_inc(new_out, 16)
            pool.dma_start(new_a_sample[:, HA - DEC_T:HA, :], outA[HA:HA + TS, :]).then_inc(new_out, 16)
            pool.dma_start(new_b_prompt, outB[0:HB, :]).then_inc(new_out, 16)
            for b in range(DEC_B):
                r = HB + DEC_T * b + DEC_T - HB
                pool.dma_start(new_b_sample[b, :, :], outB[r:r + HB, :]).then_inc(new_out, 16)
            pool.wait_ge(new_out, 16 * (3 + DEC_B))
            nc.gpsimd.iota(iota[:, :], pattern=[[1, NCAND]], base=0, channel_multiplier=0).then_inc(const_ready, 1)

            def gather_u(s, par_, k):
                at_least_apart(pool, dot_done, TOPK * s + k - 3)
                pool.indirect_dma_start(uRing[:, k % 4, :], None, peer_u,
                                        bass.IndirectOffsetOnAxis(ap=idxU[:, par_, k:k + 1], axis=0))\
                    .then_inc(u_in[k % 4], 16)

            def gather_v(s, par_, k):
                at_least_apart(pool, v_done, TOPK * s + k - 3)
                pool.indirect_dma_start(vRing[:, k % 4, :], None, peer_v,
                                        bass.IndirectOffsetOnAxis(ap=idxV[:, par_, k:k + 1], axis=0))\
                    .then_inc(v_in[k % 4], 16)

            def step(s, par_):
                at_least_apart(pool, idx_ready, s + 1)
                for k in range(TOPK):
                    gather_u(s, par_, k)
                    if k == 0:
                        at_least_apart(pool, idxv_ready, s)
                    gather_v(s - 1, 1 - par_, k)

            pool.wait_ge(scores_out, 3)
            pool.wait_ge(side_out, 8)
            pool.wait_ge(idx_ready, 1)
            for k in range(TOPK):
                gather_u(0, 0, k)
            step(1, 1)
            with pool.Fori(1, STEPS // 2) as i:
                step(2 * i, 0)
                step(2 * i + 1, 1)
            pool.wait_ge(idxv_ready, STEPS)
            for k in range(TOPK):
                gather_v(STEPS - 1, 1, k)
            pool.wait_ge(state_out, 16)

        @block.tensor
        def _(pe):
            pe.wait_ge(const_ready, 5)
            n_turned = [0]

            def turn_round(parts):
                r = n_turned[0]
                at_least(pe, turned_out, r - 1)
                for n in range(GC):
                    for src, at_ in parts(n):
                        k, m = src.shape[0], src.shape[1]
                        last = nc.tensor.transpose(ps[:, 4 * (r % 2) + n, at_:at_ + k], src, ident[0:k, 0:k])
                last.then_inc(turned, 1)
                n_turned[0] += 1

            def cols(g, n):
                return slice((GC * g + n) * P, (GC * g + n + 1) * P)

            pe.wait_ge(loaded_par, 160)
            for g in range(NG):
                turn_round(lambda n: [(parRaw[:, cols(g, n)], 0)])
            pe.wait_ge(loaded_x, 32)
            for g in range(NG):
                turn_round(lambda n: [(xRaw[:, 0, cols(g, n)], 0), (xRaw[:, 1, cols(g, n)], P),
                                      (xsRaw[:, cols(g, n)], SEQ)])
            pe.wait_ge(mod_begun, 7)

            def mod_product(slot, kc, out, last):
                for n in range(GC):
                    mm = nc.tensor.matmul(out[:, NMC * n:NMC * (n + 1)], raw[:, slot, kc % 2, n * P:(n + 1) * P],
                                          siluC[:, kc, :], start=False, stop=last and n == GC - 1,
                                          skip_group_check=True)
                return mm

            def mod_begin(out):
                nc.tensor.matmul(out, ident[:, :], zero[:, :], start=True, stop=False, skip_group_check=True)

            def mod_group(c, par_):
                out = ps[:, 4 * par_, N:N + GC * NMC]
                at_least(pe, mod_out, c - 1)
                for u in range(UNITS):
                    pe.wait_ge(raw_in[u % RING], 16 * (2 * c + u // RING + 1))
                    if u == 0:
                        mod_begin(out)
                    for kk in range(2):
                        mm = mod_product(u % RING, 2 * u + kk, out, u == UNITS - 1 and kk == 1)
                    mm.then_inc(mod_unit, 1)

            pe.wait_ge(turned_out, 8)
            mod_group(0, 0)
            mod_group(1, 1)
            pe.wait_ge(mod_out, 2)
            pe.wait_ge(loaded_state, 32)
            for g in range(NG):
                turn_round(lambda n: [(stARaw[:, 0, cols(g, n)], 0), (stARaw[:, 1, cols(g, n)], 4 * HA),
                                      (stBRaw[:, cols(g, n)], 8 * HA)])
            pe.wait_ge(turned_out, 12)
            with pe.Fori(1, PRE // 2) as i:
                mod_group(2 * i, 0)
                mod_group(2 * i + 1, 1)

            def weight_unit(c, par_, u):
                pe.wait_ge(lo_ready, UNITS * c + u + 1)
                for n in range(GC):
                    out = ps[:, 4 * par_ + n, 0:N]
                    for kk in range(2):
                        kc = 2 * u + kk
                        wh = wH[:, u % RING, kk, n * P:(n + 1) * P]
                        wl = wL[:, u % RING, kk, n * P:(n + 1) * P]
                        nc.tensor.matmul(out, wh, actH[:, kc, :], start=(kc == 0), stop=False,
                                         skip_group_check=True)
                        nc.tensor.matmul(out, wh, actL[:, kc, :], start=False, stop=False,
                                         skip_group_check=True)
                        mm = nc.tensor.matmul(out, wl, actH[:, kc, :], start=False, stop=(kc == NCH - 1),
                                              skip_group_check=True)
                mm.then_inc(mm_unit, 1)

            def in_group(c, par_):
                at_least(pe, psum_free, c - 1)
                pe.wait_ge(mod_out, PRE + c)
                out = ps[:, 4 * (1 - par_), N:N + GC * NMC]
                for j in range(PER):
                    if j in MOD_AT:
                        m = MOD_AT.index(j)
                        if m == 0:
                            at_least(pe, psum_free, c)
                            mod_begin(out)
                        pe.wait_ge(raw_in[j % RING], raw_count(c, j))
                        for kk in range(2):
                            mm = mod_product(j % RING, par_ * NCH // 2 + 2 * m + kk, out,
                                             m == GC - 1 and kk == 1)
                        mm.then_inc(mod_unit, 1)
                    else:
                        weight_unit(c, par_, main_of(j))

            for part in range(4):
                pe.wait_ge(act_lo, part + 1)
            in_group(0, 0)
            in_group(1, 1)
            with pe.Fori(1, NIN // 2) as i:
                in_group(2 * i, 0)
                in_group(2 * i + 1, 1)

            def channel_sum(src, bank, ready, count, done):
                for g in range(NG):
                    pe.wait_ge(ready, count + g + 1)
                    for n in range(GC):
                        c = GC * g + n
                        mm = nc.tensor.matmul(ps[:, bank, 0:N], ones[:, :], src[:, c, :],
                                              start=(c == 0), stop=(c == NCH - 1))
                mm.then_inc(done, 1)

            def product(w):
                def out_group(c, par_):
                    pe.wait_ge(psum_free, c - 1)
                    for u in range(UNITS):
                        if u % 2 == 0:
                            pe.wait_ge(act_lo, 4 * (w + 1) + u // 2 + 1)
                        weight_unit(c, par_, u)
                with pe.Fori(0, NG // 2) as i:
                    out_group(C_OUT + NG * w + 2 * i, 0)
                    out_group(C_OUT + NG * w + 2 * i + 1, 1)

            pe.wait_ge(psum_free, NIN)
            pe.wait_ge(mod_out, PRE + NIN)
            channel_sum(cyT, 0, conv_kept, 0, sum_done)
            pe.wait_ge(mean_ready, 1)
            product(0)
            pe.wait_ge(psum_free, C_OUT + NG)
            channel_sum(ybT, 1, squared, 0, sq_done)
            pe.wait_ge(var_ready, 1)
            product(1)
            product(2)
            pe.wait_ge(psum_free, C_OUT + 3 * NG)
            channel_sum(xT, 0, psum_free, C_OUT + 2 * NG, sum_done)

            def side(jobs, m, bank):
                for c in range(NCH):
                    last = nc.tensor.transpose(ps[0:m, bank + c // GC, (c % GC) * P:(c % GC + 1) * P],
                                               jobs(c), ident[:, :])
                last.then_inc(side_turned, 1)

            pe.wait_ge(key_in, 16)
            side(lambda c: keyRaw[:, c, :], P, 4)
            pe.wait_ge(mean_ready, 2)
            pe.wait_ge(tail_back, 16)
            pe.wait_ge(side_out, 1)
            side(lambda c: tails[:, c, 0:HA + TS], HA + TS, 4)
            pe.wait_ge(side_out, 2)
            side(lambda c: tails[:, c, HA + TS:96], HB + TS, 4)
            channel_sum(ybT, 1, squared, 4, sq_done)
            pe.wait_ge(var_ready, 2)
            pe.wait_ge(side_out, 3)
            product(3)
            pe.wait_ge(psum_free, C_OUT + 4 * NG)

            def score(s, bank):
                at_ = (s % 2) * 2 * NKEYS
                for side_ in range(2):
                    o = at_ + side_ * NKEYS
                    if s < 2:
                        for r in range(4):
                            hs = 2 * (2 * r + s) + side_
                            mm = nc.tensor.matmul(ps[32 * r:32 * r + TS, bank, o:o + NKEYS], cyT[:, hs, SEQ:N],
                                                  keyT[:, hs, :], start=True, stop=True)
                    else:
                        t, h = (s - 2) // HEADS, (s - 2) % HEADS
                        hs = 2 * h + side_
                        mm = nc.tensor.matmul(ps[:, bank, o:o + NKEYS], cyT[:, hs, t * P:(t + 1) * P],
                                              keyT[:, hs, :], start=True, stop=True)
                return mm

            for rnd, (first, count) in enumerate([(0, 8), (8, 8), (16, 2)]):
                if rnd == 2:
                    pe.wait_ge(scores_out, 1)
                for s in range(first, first + count):
                    mm = score(s, 4 * (rnd % 2) + (s - first) // 2)
                mm.then_inc(scored, 1)

            def turn_u2(t):
                for c in range(NCH):
                    src = u2Rep[:, c, :] if t == 0 else ybT[:, c, (t - 1) * P:t * P]
                    last = nc.tensor.transpose(ps[:, c // GC, (c % GC) * P:(c % GC + 1) * P], src, ident[:, :])
                last.then_inc(u2_ready, 1)

            pe.wait_ge(scores_out, 3)
            pe.wait_ge(rep_ready, 3)
            turn_u2(0)
            jobs = [(lambda c: xT[:, c, SEQ:N], TS), (lambda c: xT[:, c, 0:P], P),
                    (lambda c: xT[:, c, P:2 * P], P), (lambda c: g2pRep[:, c, :], P),
                    (lambda c: g2sRep[:, c, :], TS)]
            for n, (job, m) in enumerate(jobs):
                pe.wait_ge(side_out, 3 + n)
                side(job, m, 4)
            pe.wait_ge(side_out, 8)

            def add_experts(s, first):
                for k in range(TOPK):
                    pe.wait_ge(diag_ready, TOPK * s + k + 1)
                    pe.wait_ge(v_in[k % 4], 16 * (4 * s + k // 4 + 1))
                    for n in range(4):
                        mm = nc.tensor.matmul(ps[:, 4 + n, :], diag[:, k, :], vRing[:, k % 4, n * 512:(n + 1) * 512],
                                              start=(first and k == 0), stop=True, skip_group_check=True)
                    mm.then_inc(v_done, 1)

            for t, (a, b) in enumerate(TILES):
                if t == 1:
                    pe.wait_ge(fs_ready, 1)
                    for n in range(4):
                        mm = nc.tensor.matmul(ps[0:TS, 4 + n, :], fold[:, :], fin[:, n * 512:(n + 1) * 512],
                                              start=True, stop=True)
                    mm.then_inc(folded, 1)
                at_least(pe, f_free, t)
                add_experts(a, True)
                if b - a > 1:
                    with pe.Fori(a + 1, b) as s:
                        add_experts(s, False)
                if t < 2:
                    pe.wait_ge(dot_done, TOPK * (b + 1))
                    turn_u2(t + 1)
                add_experts(b, False)

        @block.scalar
        def _(act):
            chain = Chain(act, a_chain)
            act.wait_ge(turned_out, 4)
            nc.scalar.activation(siluC[:, :, :], par[:, :, R_C:R_C + NMC], ACT.Silu).then_inc(mod_begun, 1)

            def split(n, src, ready, count, mm):
                at_least(act, mm_unit, mm)
                for k in range(4):
                    act.wait_ge(ready, count + k + 1)
                    nc.scalar.activation(actH[:, GC * k:GC * k + GC, :], src[:, GC * k:GC * k + GC, :],
                                         ACT.Copy).then_inc(act_hi, 1)

            def weights(c, u, slot, count):
                act.wait_ge(raw_in[slot], count)
                at_least_apart(act, mm_unit, UNITS * c + u - RING + 1)
                nc.scalar.activation(wH[:, u % RING], raw[:, slot], ACT.Copy).then_inc(hi_ready, 1)

            split(0, ybT, src_ready, 0, 0)
            nc.scalar.activation(xT[:, :, :], xT[:, :, :], ACT.Copy, scale=ALPHA).then_inc(x_scaled, 1)

            def evacuate(g, q):
                c = NQ * g + q
                if ORDER[q] in (A_VAL, H_IN, B_GATE):
                    return
                act.wait_ge(mm_unit, UNITS * (c + 1))
                at_least_apart(act, psum_free, c)
                if ORDER[q] == A_GATE:
                    out, f = tmp[:, :, :], ACT.Sigmoid
                elif ORDER[q] == C_GATE:
                    out, f = tmp[:, :, :], ACT.Copy
                else:
                    gate = sgA if ORDER[q] == GATE_A else sgB
                    out, f = gate[:, bass.ds(g * GC, GC), :], ACT.Sigmoid
                nc.scalar.activation(out, group(c), f).then_inc(psum_free, 1)

            def keep_conv(g):
                at_least_apart(act, conv_done, g + 1)
                nc.scalar.activation(cyT[:, bass.ds(g * GC, GC), :], acc[:, :, :], ACT.Copy).then_inc(conv_kept, 1)

            def in_groups(g, first):
                for q in range(NQ):
                    c = NQ * g + q
                    for j in range(PER):
                        u = main_of(j)
                        if u is None:
                            continue
                        if u == 3:
                            if q > 0:
                                evacuate(g, q - 1)
                            elif not first:
                                evacuate(g - 1, NQ - 1)
                        weights(c, u, j % RING, raw_count(c, j))
                        if q == 1 and u == 1 and not first:
                            keep_conv(g - 1)
                        if q == 5 and u == 5:
                            if not first:
                                at_least_apart(act, tail_saved, 16 * g)
                            at_least_apart(act, psum_free, NQ * g + 4)
                            chain.restart()
                            for at_, src in ((0, gluP[:, :, SEQ:SEQ + HA]), (HA + TS, cbP[:, :, SEQ:SEQ + HB])):
                                chain.link(nc.scalar.activation(tail[:, :, at_:at_ + src.shape[2]], src, ACT.Copy))
                            chain.link(nc.scalar.activation(
                                tail[:, :, HA:HA + TS].rearrange("p n (b t) -> p n b t", b=DEC_B),
                                gluS[:, :, :, HA:HA + DEC_T], ACT.Copy))
                            chain.all()
                            nc.scalar.activation(
                                tail[:, :, 96 - TS:96].rearrange("p n (b t) -> p n b t", b=DEC_B),
                                cbS[:, :, :, HB:HB + DEC_T], ACT.Copy).then_inc(tail_ready, 1)

            in_groups(0, True)
            with act.Fori(1, NG) as g:
                in_groups(g, False)
            evacuate(NG - 1, NQ - 1)
            keep_conv(NG - 1)

            def product(w, hook, evac=None):
                def out_group(i, first):
                    c = C_OUT + NG * w + i
                    for u in range(UNITS):
                        weights(c, u, u % RING, raw_count_out(c, u))
                        if u == 3:
                            if first:
                                hook()
                            elif evac:
                                evac(i - 1)
                out_group(0, True)
                with act.Fori(1, NG) as i:
                    out_group(i, False)
                if evac:
                    evac(NG - 1)

            def take_mean(n):
                act.wait_ge(sum_done, n)
                if n == 1:
                    act.wait_ge(tail_saved, 16 * NG)
                nc.scalar.activation(mean[:, :], ps[:, 0, 0:N], ACT.Copy, scale=1.0 / D).then_inc(mean_ready, 1)

            def squares(src, n):
                for k in range(4):
                    act.wait_ge(centred, 4 * n + k + 1)
                    nc.scalar.activation(ybT[:, GC * k:GC * k + GC, :], src[:, GC * k:GC * k + GC, :],
                                         ACT.Square).then_inc(squared, 1)

            def deviation(n):
                act.wait_ge(var_ready, n + 1)
                nc.scalar.activation(rstd[:, :], rstd[:, :], ACT.Sqrt).then_inc(sd_ready, 1)

            def apply(src, n, f, rg, rb):
                for c in range(NCH):
                    if c % GC == 0:
                        act.wait_ge(normed, 4 * n + c // GC + 1)
                    a = nc.scalar.activation(src[:, c, :], src[:, c, :], f, scale=par[:, c, rg:rg + 1],
                                             bias=par[:, c, rb:rb + 1])
                    a.then_inc(affine, 1)

            split(1, ybT, src_ready, 4, UNITS * NIN)
            take_mean(1)

            def square_a():
                act.wait_ge(act_lo, 8)
                squares(cyT, 0)

            product(0, square_a)
            deviation(0)
            apply(cyT, 0, ACT.Silu, R_AG, R_AB)

            def split_after(n, src, ready, counts, mm):
                at_least(act, mm_unit, mm)
                for k in range(4):
                    act.wait_ge(ready, counts[k])
                    nc.scalar.activation(actH[:, GC * k:GC * k + GC, :], src[:, GC * k:GC * k + GC, :],
                                         ACT.Copy).then_inc(act_hi, 1)

            split_after(2, cyT, affine, [4, 8, 12, 16], UNITS * (C_OUT + NG))
            product(1, lambda: None)
            split_after(3, sgA, psum_free, [C_OUT + NG + k + 1 for k in range(4)], UNITS * (C_OUT + 2 * NG))
            product(2, lambda: None)
            take_mean(2)

            def rows(t):
                return t.rearrange("p (b n) -> p b n", b=4)

            def side_copy(n, out, src, scale=1.0):
                act.wait_ge(side_turned, n)
                nc.scalar.activation(out, src, ACT.Copy, scale=scale).then_inc(side_out, 1)

            squares(xT, 1)
            side_copy(1, keyT[:, :, :].rearrange("p (b a) k -> p b (a k)", b=4), ps[:, 4:8, :])
            side_copy(2, rows(outA[:, :]), ps[0:HA + TS, 4:8, :])
            side_copy(3, rows(outB[:, :]), ps[0:HB + TS, 4:8, :])
            deviation(1)
            apply(xT, 1, ACT.Identity, R_1G, R_1B)
            split(4, ybT, src_ready, 8, UNITS * (C_OUT + 3 * NG))

            def queries(i):
                c = C_OUT + 3 * NG + i
                act.wait_ge(mm_unit, UNITS * (c + 1))
                at_least_apart(act, psum_free, c)
                nc.scalar.activation(cyT[:, bass.ds(i * GC, GC), :], group(c), ACT.Copy).then_inc(psum_free, 1)

            product(3, lambda: None, queries)

            act.wait_ge(new_out, 16 * (3 + DEC_B))
            for rnd, (first, count) in enumerate([(0, 8), (8, 8), (16, 2)]):
                act.wait_ge(scored, rnd + 1)
                b = 4 * (rnd % 2)
                nc.scalar.activation(
                    scores[:, first:first + count].rearrange("p (b e) s k -> p b (e s k)", e=2),
                    ps[:, b:b + count // 2, :], ACT.Copy).then_inc(scores_out, 1)
            for r in range(4):
                a = nc.scalar.activation(u2Rep[:, :, TS * r:TS * r + TS], ybT[:, :, SEQ:N], ACT.Copy)
                if r < 3:
                    chain.link(a)
            chain.all()
            a.then_inc(rep_ready, 1)
            nc.scalar.activation(g2pRep[:, :, :], modT[:, G2 * NCH:(G2 + 1) * NCH, 0:1].broadcast_to((P, NCH, P)),
                                 ACT.Copy).then_inc(rep_ready, 1)
            for b in range(DEC_B):
                a = nc.scalar.activation(
                    g2sRep[:, :, DEC_T * b:DEC_T * b + DEC_T],
                    modT[:, G2 * NCH:(G2 + 1) * NCH, 1 + b:2 + b].broadcast_to((P, NCH, DEC_T)), ACT.Copy)
                if b < DEC_B - 1:
                    chain.link(a)
            chain.all()
            a.then_inc(rep_ready, 1)

            side_copy(4, rows(x1Tok[0:TS, 0, :]), ps[0:TS, 4:8, :], ALPHA)
            side_copy(5, rows(x1Tok[:, 1, :]), ps[:, 4:8, :], ALPHA)
            side_copy(6, rows(x1Tok[:, 2, :]), ps[:, 4:8, :], ALPHA)
            side_copy(7, rows(g2P[:, :]), ps[:, 4:8, :])
            side_copy(8, rows(g2S[:, :]), ps[0:TS, 4:8, :])

            def step(s, par_, first=False):
                at_least_apart(act, dot_done, TOPK * (s + 1))
                nc.scalar.activation(gel[:, :], dots[:, par_, :], ACT.Gelu).then_inc(act_done, 1)
                nc.scalar.activation(ex[:, :], best[:, par_, :], ACT.Exp, bias=negMax[:, par_:par_ + 1],
                                     accum_out=exSum[:, :]).then_inc(act_done, 1)
                at_least_apart(act, wts_ready, s + 1)
                for k in range(TOPK):
                    if not first:
                        at_least_apart(act, v_done, TOPK * (s - 1) + k + 1)
                    nc.scalar.activation(diag[:, k, :], ident[:, :], ACT.Copy,
                                         scale=wts[:, par_, k:k + 1]).then_inc(diag_ready, 1)

            def deviation2(t):
                act.wait_ge(ve_ready, t + 1)
                m = ROWS[t]
                nc.scalar.activation(ve[0:m, 1:2], ve[0:m, 0:1], ACT.Sqrt).then_inc(sdev_ready, 1)

            act.wait_ge(side_turned, 7)
            for t, (a, b) in enumerate(TILES):
                step(a, 0, t == 0)
                if t > 0:
                    deviation2(t - 1)
                step(a + 1, 1)
                if b - a > 1:
                    with act.Fori(0, (b - a - 1) // 2) as i:
                        step(a + 2 + 2 * i, 0)
                        step(a + 3 + 2 * i, 1)
            deviation2(2)

        @block.vector
        def _(dve):
            chain = Chain(dve, v_chain)
            V = nc.vector

            def copy_round(r, outs):
                dve.wait_ge(turned, r + 1)
                for n, (out, src) in enumerate(outs):
                    i = V.tensor_copy(out, src)
                    if n < len(outs) - 1:
                        chain.link(i)
                        chain.all()
                i.then_inc(turned_out, 1)

            def bset(r):
                return slice(4 * (r % 2), 4 * (r % 2) + 4)

            for g in range(NG):
                copy_round(g, [(par[:, GC * g:GC * g + GC, :], ps[:, bset(g), 0:NROW])])
            dve.wait_ge(turned_out, 4)
            for s in range(6):
                V.tensor_scalar(modT[:, s * NCH:(s + 1) * NCH, :],
                                par[:, :, R_MOD + s:R_MOD + s + 1].broadcast_to((P, NCH, NMC)),
                                1.0 if s in (SC1, G1, SC2, G2) else 0.0, None, ALU.add).then_inc(mod_begun, 1)
            dve.wait_ge(mod_begun, 7)
            for g in range(NG):
                copy_round(4 + g, [(xT[:, GC * g:GC * g + GC, :], ps[:, bset(g), 0:N])])

            def pre_mod(c, par_):
                at_least_apart(dve, mod_unit, UNITS * (c + 1))
                at_ = modT[:, bass.ds(c * GC, GC), :]
                src = ps[:, 4 * par_, N:N + GC * NMC].rearrange("p (n r) -> p n r", n=GC)
                V.tensor_tensor(at_, at_, src, ALU.add).then_inc(mod_out, 1)

            pre_mod(0, 0)
            pre_mod(1, 1)
            cyA = cyT[:, :, :].rearrange("p (g n) t -> p g (n t)", g=NG)
            for g in range(NG):
                copy_round(8 + g, [
                    (cyA[:, g, 0:GC * 8 * HA].rearrange("p (n t) -> p n t", n=GC), ps[:, bset(g), 0:8 * HA]),
                    (cyA[:, g, GC * 8 * HA:GC * 8 * (HA + HB)].rearrange("p (n t) -> p n t", n=GC),
                     ps[:, bset(g), 8 * HA:8 * (HA + HB)])])
            with dve.Fori(1, PRE // 2) as i:
                pre_mod(2 * i, 0)
                pre_mod(2 * i + 1, 1)

            def tokens4(t):
                return t.rearrange("p c (b t) -> p c b t", b=DEC_B)

            def modulate(src, sh, sc):
                c0, c1 = sc * NCH, sh * NCH
                for k in range(4):
                    part = slice(GC * k, GC * k + GC)
                    for c in range(GC * k, GC * k + GC):
                        chain.link(V.tensor_scalar(ybT[:, c, 0:SEQ], src[:, c, 0:SEQ], modT[:, c0 + c, 0:1],
                                                   modT[:, c1 + c, 0:1], ALU.mult, ALU.add))
                    by = modT[:, c0 + GC * k:c0 + GC * k + GC, 1:NMC].unsqueeze(3).broadcast_to((P, GC, DEC_B, DEC_T))
                    off = modT[:, c1 + GC * k:c1 + GC * k + GC, 1:NMC].unsqueeze(3).broadcast_to((P, GC, DEC_B, DEC_T))
                    out = tokens4(ybT[:, part, SEQ:N])
                    chain.link(V.tensor_tensor(out, tokens4(src[:, part, SEQ:N]), by, ALU.mult))
                    chain.all()
                    V.tensor_tensor(out, out, off, ALU.add).then_inc(src_ready, 1)

            def split_low(n, src):
                for k in range(4):
                    part = slice(GC * k, GC * k + GC)
                    dve.wait_ge(act_hi, 4 * n + k + 1)
                    V.tensor_tensor(actL[:, part, :], src[:, part, :], actH[:, part, :].bitcast(F32),
                                    ALU.subtract).then_inc(act_lo, 1)

            dve.wait_ge(turned_out, 12)
            dve.wait_ge(mod_out, PRE)
            modulate(xT, SH1, SC1)
            split_low(0, ybT)

            def weights(c, u, slot):
                at_least_apart(dve, hi_ready, UNITS * c + u + 1)
                V.tensor_tensor(wL[:, u % RING], raw[:, slot], wH[:, u % RING].bitcast(F32),
                                ALU.subtract).then_inc(lo_ready, 1)

            def in_mod(c):
                at_least_apart(dve, mod_unit, MODS + GC * (c + 1))
                at_ = modT[:, bass.ds((PRE + (c // 2)) * GC, GC), :]
                at_least_apart(dve, mod_out, PRE + c)
                V.tensor_tensor(at_, at_, mod_bank(c), ALU.add).then_inc(mod_out, 1)

            def evacuate(g, q):
                c = NQ * g + q
                if ORDER[q] not in (A_VAL, H_IN, B_GATE):
                    return
                at_least_apart(dve, mm_unit, UNITS * (c + 1))
                at_least_apart(dve, psum_free, c)
                if ORDER[q] == B_GATE:
                    V.tensor_tensor(ybT[:, bass.ds(g * GC, GC), :], group(c), tmp[:, :, :], ALU.mult)\
                     .then_inc(psum_free, 1)
                    at_least_apart(dve, psum_free, c + 1)
                    return
                toP, toS, h = (gluP, gluS, HA) if ORDER[q] == A_VAL else (cbP, cbS, HB)
                chain.link(V.tensor_tensor(toP[:, :, h:h + SEQ], group(c, 0, SEQ), tmp[:, :, 0:SEQ], ALU.mult))
                chain.all()
                for n in range(GC):
                    i = V.tensor_tensor(toS[:, n, :, h:h + DEC_T],
                                        ps[:, bass.ds(bank_set(c) + n, 1), SEQ:N].rearrange("p a (b t) -> p (a b) t", b=DEC_B),
                                        tmp[:, n, SEQ:N].rearrange("p (b t) -> p b t", b=DEC_B), ALU.mult)
                    if n < GC - 1:
                        chain.link(i)
                        chain.all()
                i.then_inc(psum_free, 1)
                at_least_apart(dve, psum_free, c + 1)

            def s4(t):
                return t.rearrange("p (b t) -> p b t", b=DEC_B)

            def conv_tap(j):
                for n in range(GC):
                    for lo, out, src in ((0, acc[:, n, 0:SEQ], gluP[:, n, j:j + SEQ]),
                                         (1, s4(acc[:, n, SEQ:N]), gluS[:, n, :, j:j + DEC_T])):
                        w = wAg[:, n, j:j + 1]
                        if j == 0:
                            chain.link(V.tensor_scalar(out, src, w, wBg[:, n, WB:WB + 1], ALU.mult, ALU.add))
                        else:
                            chain.back(2 * GC - 1)
                            chain.link(V.scalar_tensor_tensor(out=out, in0=src, scalar=w, in1=out,
                                                              op0=ALU.mult, op1=ALU.add))

            def conv_b():
                for j in range(WB):
                    for n in range(GC):
                        for out, src in ((tmp[:, n, 0:SEQ], cbP[:, n, j:j + SEQ]),
                                         (s4(tmp[:, n, SEQ:N]), cbS[:, n, :, j:j + DEC_T])):
                            w = wBg[:, n, j:j + 1]
                            if j == 0:
                                chain.link(V.tensor_scalar(out, src, w, None, ALU.mult))
                            else:
                                chain.back(2 * GC - 1)
                                chain.link(V.scalar_tensor_tensor(out=out, in0=src, scalar=w, in1=out,
                                                                  op0=ALU.mult, op1=ALU.add))
                chain.all()

            def begin_group(g, first):
                if not first:
                    at_least_apart(dve, tail_ready, g)
                one = cyA[:, bass.ds(g, 1), :]
                for n in range(GC):
                    chain.link(V.tensor_copy(
                        gluS[:, n, :, 0:HA],
                        one[:, :, n * 8 * HA:(n + 1) * 8 * HA].rearrange("p g (b r) -> p (g b) r", b=DEC_B)))
                    chain.link(V.tensor_copy(
                        cbS[:, n, :, 0:HB],
                        one[:, :, GC * 8 * HA + n * 8 * HB:GC * 8 * HA + (n + 1) * 8 * HB]
                        .rearrange("p g (b r) -> p (g b) r", b=DEC_B)))
                chain.link(V.tensor_copy(wAg[:, :, :], par[:, bass.ds(g * GC, GC), R_WA:R_WA + WA]))
                chain.link(V.tensor_copy(wBg[:, :, :], par[:, bass.ds(g * GC, GC), R_WB:R_WB + WB + 1]))
                chain.all()

            def in_groups(g, first):
                chain.restart()
                tap = 0
                for q in range(NQ):
                    c = NQ * g + q
                    for j in range(PER):
                        u = main_of(j)
                        if u is None:
                            continue
                        if u == 3:
                            if q > 0:
                                in_mod(c - 1)
                                evacuate(g, q - 1)
                            elif not first:
                                in_mod(c - 1)
                        weights(c, u, j % RING)
                        if q == 0 and u == 5:
                            begin_group(g, first)
                        if q == 4 and u == 4:
                            conv_b()
                        if (q > 2 or q == 2 and u >= 4) and tap < WA and not (q == 4 and u == 4):
                            if tap == 0 and not first:
                                at_least_apart(dve, conv_kept, g)
                            conv_tap(tap)
                            tap += 1
                            if tap == WA:
                                chain.all()
                                dve.nop(nofuse=True).then_inc(conv_done, 1)

            dve.wait_ge(x_scaled, 1)
            in_groups(0, True)
            with dve.Fori(1, NG) as g:
                in_groups(g, False)
            in_mod(NIN - 1)
            chain.restart()

            def product(w, hook, evac):
                def out_group(i, first):
                    c = C_OUT + NG * w + i
                    for u in range(UNITS):
                        weights(c, u, u % RING)
                        if u == 3:
                            if first:
                                hook()
                            else:
                                evac(i - 1)
                out_group(0, True)
                with dve.Fori(1, NG) as i:
                    chain.restart()
                    out_group(i, False)
                    chain.all()
                chain.restart()
                evac(NG - 1)

            def ready(c):
                at_least_apart(dve, mm_unit, UNITS * (c + 1))
                at_least_apart(dve, psum_free, c)

            def centre(src, n):
                dve.wait_ge(mean_ready, n + 1)
                for k in range(4):
                    part = src[:, GC * k:GC * k + GC, :]
                    V.tensor_tensor(part, part, mean[:, :].unsqueeze(1).broadcast_to((P, GC, N)),
                                    ALU.subtract).then_inc(centred, 1)

            def normalise(src, n, bank):
                dve.wait_ge(sq_done, n + 1)
                V.tensor_scalar(rstd[:, :], ps[:, bank, 0:N], 1.0 / D, EPS, ALU.mult, ALU.add).then_inc(var_ready, 1)
                dve.wait_ge(sd_ready, n + 1)
                chain.link(V.reciprocal(rstd[:, :], rstd[:, :]))
                chain.all()
                for k in range(4):
                    part = src[:, GC * k:GC * k + GC, :]
                    V.tensor_tensor(part, part, rstd[:, :].unsqueeze(1).broadcast_to((P, GC, N)),
                                    ALU.mult).then_inc(normed, 1)

            for k in range(4):
                dve.nop(nofuse=True).then_inc(src_ready, 1)
            split_low(1, ybT)

            def gate_b(i):
                c = C_OUT + i
                ready(c)
                g_ = sgB[:, bass.ds(i * GC, GC), :]
                V.tensor_tensor(g_, group(c), g_, ALU.mult).then_inc(psum_free, 1)

            product(0, lambda: centre(cyT, 0), gate_b)
            normalise(cyT, 0, 1)
            for k in range(4):
                dve.wait_ge(affine, 4 * (k + 1))
                dve.wait_ge(act_hi, 8 + k + 1)
                V.tensor_tensor(actL[:, GC * k:GC * k + GC, :], cyT[:, GC * k:GC * k + GC, :],
                                actH[:, GC * k:GC * k + GC, :].bitcast(F32), ALU.subtract).then_inc(act_lo, 1)

            def gate_a(i):
                c = C_OUT + NG + i
                ready(c)
                g_ = sgA[:, bass.ds(i * GC, GC), :]
                chain.link(V.tensor_tensor(g_, group(c), g_, ALU.mult))
                chain.all()
                V.tensor_tensor(g_, g_, sgB[:, bass.ds(i * GC, GC), :], ALU.add).then_inc(psum_free, 1)

            product(1, lambda: None, gate_a)
            dve.wait_ge(psum_free, C_OUT + 2 * NG)
            dve.nop(nofuse=True).then_inc(gates_done, 1)
            split_low(3, sgA)

            def residual(i):
                c = C_OUT + 2 * NG + i
                ready(c)
                by = modT[:, bass.ds(G1 * NCH + i * GC, GC), :]
                chain.link(V.tensor_tensor(sampleM[:, :, :, :],
                                           ps[:, bass.ds(bank_set(c), 4), SEQ:N].rearrange("p n (b t) -> p n b t", b=DEC_B),
                                           by[:, :, 1:NMC].unsqueeze(3).broadcast_to((P, GC, DEC_B, DEC_T)), ALU.mult))
                for n in range(GC):
                    xs_ = xT[:, bass.ds(i * GC + n, 1), 0:SEQ].rearrange("p a t -> p (a t)")
                    src = ps[:, bass.ds(bank_set(c) + n, 1), 0:SEQ].rearrange("p a t -> p (a t)")
                    sc_ = modT[:, bass.ds(G1 * NCH + i * GC + n, 1), 0:1].rearrange("p a t -> p (a t)")
                    chain.link(V.scalar_tensor_tensor(out=xs_, in0=src, scalar=sc_, in1=xs_,
                                                      op0=ALU.mult, op1=ALU.add))
                chain.all()
                xs_ = xT[:, bass.ds(i * GC, GC), SEQ:N]
                V.tensor_tensor(xs_, xs_, sampleM[:, :, :, :].rearrange("p n b t -> p n (b t)"), ALU.add)\
                 .then_inc(psum_free, 1)

            product(2, lambda: None, residual)
            dve.wait_ge(psum_free, C_OUT + 3 * NG)
            centre(xT, 1)
            normalise(xT, 1, 1)
            dve.wait_ge(affine, 2 * NCH)
            modulate(xT, SH2, SC2)
            split_low(4, ybT)

            def product_q():
                def out_group(i):
                    for u in range(UNITS):
                        weights(C_OUT + 3 * NG + i, u, u % RING)
                with dve.Fori(0, NG) as i:
                    out_group(i)

            product_q()
            chain.restart()

            dve.wait_ge(const_ready, 6)
            chain.link(V.tensor_copy(iotaF[:, :], iota[:, :]))
            chain.link(V.tensor_tensor(fold[:, :], ident[:, 0:TS], ident[:, TS:2 * TS], ALU.add))
            for r in range(2, 4):
                chain.all()
                chain.link(V.tensor_tensor(fold[:, :], fold[:, :], ident[:, TS * r:TS * r + TS], ALU.add))
            chain.all()

            def top16(vals, src, spare, index):
                jobs = list(zip(vals, src, spare, index))
                for v, a, b, x in jobs:
                    chain.link(V.max(v[:, 0:8], a))
                for v, a, b, x in jobs:
                    chain.back(len(jobs) - 1)
                    chain.link(V.max_index(x[:, 0:8], v[:, 0:8], a))
                    chain.link(V.match_replace(b, v[:, 0:8], a, LOWEST))
                chain.all()
                for v, a, b, x in jobs:
                    chain.link(V.max(v[:, 8:16], b))
                chain.all()
                for v, a, b, x in jobs:
                    chain.link(V.max_index(x[:, 8:16], v[:, 8:16], b))
                chain.all()

            def route(s, par_):
                chain.link(V.tensor_copy(sc0[:, :, :], scores[:, bass.ds(s, 1), :, :].rearrange("p a s k -> p (a s) k")))
                chain.all()
                top16([top[:, 0, :], top[:, 1, :]], [sc0[:, 0, :], sc0[:, 1, :]],
                      [sc1[:, 0, :], sc1[:, 1, :]], [topIx[:, 0, :], topIx[:, 1, :]])
                chain.link(V.tensor_scalar(topIxF[:, 0, :], topIx[:, 0, :], float(NKEYS), None, ALU.mult))
                chain.link(V.tensor_copy(topIxF[:, 1, :], topIx[:, 1, :]))
                chain.all()
                for out, src in ((cand, top), (candId, topIxF)):
                    o = 0
                    for i, r, n in BLOCKS:
                        chain.link(V.tensor_tensor(
                            out[:, o:o + r * n].rearrange("p (r n) -> p r n", r=r),
                            src[:, 0, i:i + r].unsqueeze(2).broadcast_to((P, r, n)),
                            src[:, 1, 0:n].unsqueeze(1).broadcast_to((P, r, n)), ALU.add))
                        o += r * n
                chain.all()
                top16([best[:, par_, :]], [cand[:, :]], [cand2[:, :]], [pos[:, :]])
                chain.link(V.tensor_copy(posF[:, :], pos[:, :]))
                chain.link(V.tensor_scalar(negMax[:, par_:par_ + 1], best[:, par_, 0:1], -1.0, None, ALU.mult))
                chain.all()
                chain.link(V.tensor_tensor(onehot[:, :, :], iotaF[:, :].unsqueeze(1).broadcast_to((P, TOPK, NCAND)),
                                           posF[:, :].unsqueeze(2).broadcast_to((P, TOPK, NCAND)), ALU.is_equal))
                chain.all()
                chain.link(V.tensor_tensor(onehot[:, :, :], onehot[:, :, :],
                                           candId[:, :].unsqueeze(1).broadcast_to((P, TOPK, NCAND)), ALU.mult))
                chain.all()
                chain.link(V.reduce_sum(eidF[:, :], onehot[:, :, :], AX.X))
                chain.all()
                V.tensor_copy(idxU[:, par_, :], eidF[:, :]).then_inc(idx_ready, 1)

            def step(s, par_, more=True):
                chain.restart()
                if more:
                    route(s + 1, 1 - par_)
                for k in range(TOPK):
                    at_least_apart(dve, u_in[k % 4], 16 * (4 * s + k // 4 + 1))
                    row = uRing[:, k % 4, :]
                    V.scalar_tensor_tensor(out=row, in0=row, scalar=1.0, in1=ps[:, 0:4, :].rearrange("p b n -> p (b n)"),
                                           op0=ALU.mult, op1=ALU.mult,
                                           accum_out=dots[:, par_, k:k + 1]).then_inc(dot_done, 1)
                at_least_apart(dve, act_done, 2 * (s + 1))
                chain.link(V.reciprocal(exInv[:, :], exSum[:, :]))
                chain.link(V.tensor_tensor(ex[:, :], ex[:, :], gel[:, :], ALU.mult))
                chain.all()
                V.tensor_scalar(wts[:, par_, :], ex[:, :], exInv[:, :], None, ALU.mult).then_inc(wts_ready, 1)
                V.tensor_copy(idxV[:, par_, :], idxU[:, par_, :]).then_inc(idxv_ready, 1)
                at_least_apart(dve, wts_ready, s + 1)
                at_least_apart(dve, idxv_ready, s + 1)

            def finish(t):
                m = ROWS[t]
                dve.wait_ge(v_done, TOPK * (TILES[t][1] + 1))
                at_least(dve, y_out, 16 * t)
                f = fin[0:m, :]
                if t == 0:
                    V.tensor_copy(fin[:, :], ps[:, 4:8, :].rearrange("p b n -> p (b n)")).then_inc(fs_ready, 1)
                    dve.wait_ge(folded, 1)
                V.tensor_tensor(f, ps[0:m, 4:8, :].rearrange("p b n -> p (b n)"), (g2S if t == 0 else g2P)[0:m, :],
                                ALU.mult).then_inc(f_free, 1)
                dve.wait_ge(f_free, t + 1)
                chain.link(V.tensor_tensor(f, f, x1Tok[0:m, t, :], ALU.add))
                chain.all()
                for n in range(4):
                    chain.link(V.bn_stats(stats[0:m, n, :], fin[0:m, n * 512:(n + 1) * 512]))
                chain.all()
                chain.link(V.bn_aggr(mv[0:m, :], stats[0:m, :, :].rearrange("p a b -> p (a b)")))
                chain.all()
                V.tensor_scalar(ve[0:m, 0:1], mv[0:m, 1:2], EPS, None, ALU.add).then_inc(ve_ready, 1)
                dve.wait_ge(sdev_ready, t + 1)
                chain.link(V.reciprocal(ve[0:m, 2:3], ve[0:m, 1:2]))
                chain.all()
                chain.link(V.tensor_scalar(f, f, mv[0:m, 0:1], ve[0:m, 2:3], ALU.subtract, ALU.mult))
                chain.all()
                chain.link(V.tensor_tensor(f, f, lnG[0:m, :], ALU.mult))
                chain.all()
                V.tensor_tensor(f, f, lnB[0:m, :], ALU.add).then_inc(y_ready, 1)

            dve.wait_ge(scores_out, 3)
            route(0, 0)
            dve.wait_ge(ln_in, 32)
            for t, (a, b) in enumerate(TILES):
                dve.wait_ge(u2_ready, t + 1)
                step(a, 0)
                if t > 0:
                    finish(t - 1)
                step(a + 1, 1)
                if t < 2 and b - a > 1:
                    with dve.Fori(0, (b - a - 1) // 2) as i:
                        step(a + 2 + 2 * i, 0)
                        step(a + 3 + 2 * i, 1)
                if t == 2:
                    with dve.Fori(0, (b - a - 3) // 2) as i:
                        step(a + 2 + 2 * i, 0)
                        step(a + 3 + 2 * i, 1)
                    step(b - 1, 0)
                    step(b, 1, more=False)
            chain.restart()
            finish(2)
            dve.wait_ge(y_ready, 3)


def kernel(**inputs):
    import numpy as np
    import concourse.bacc as bacc
    from concourse.bass_utils import run_bass_kernel_spmd

    rows = lambda a: a.reshape(-1, a.shape[-1])
    b_mod = np.asarray(inputs["b_mod"])
    arrays = {
        "x_prompt": rows(np.asarray(inputs["x_prompt"])), "x_sample": rows(np.asarray(inputs["x_sample"])),
        "state_a": rows(np.asarray(inputs["state_conv_a"])), "state_b": rows(np.asarray(inputs["state_conv_b"])),
        "c_prompt": np.asarray(inputs["c_prompt"]), "c_sample": np.asarray(inputs["c_sample"]),
        "w_mod": np.asarray(inputs["w_mod"])[0], "b_mod": b_mod.reshape(6, -1),
        "w_in": np.asarray(inputs["w_in"])[0], "conv_a_w": np.asarray(inputs["conv_a_w"])[0],
        "conv_a_b": np.asarray(inputs["conv_a_b"]), "ln_a_g": np.asarray(inputs["ln_a_g"]),
        "ln_a_b": np.asarray(inputs["ln_a_b"]), "w_a_out": np.asarray(inputs["w_a_out"])[0],
        "conv_b_w": np.asarray(inputs["conv_b_w"])[0], "w_b_out": np.asarray(inputs["w_b_out"])[0],
        "w_o": np.asarray(inputs["w_o"])[0], "ln1_g": np.asarray(inputs["ln1_g"]),
        "ln1_b": np.asarray(inputs["ln1_b"]), "w_q": np.asarray(inputs["w_q"])[0],
        "sub_keys": np.asarray(inputs["sub_keys"])[0], "peer_u": np.asarray(inputs["peer_u"])[0],
        "peer_v": np.asarray(inputs["peer_v"])[0], "ln2_g": np.asarray(inputs["ln2_g"]),
        "ln2_b": np.asarray(inputs["ln2_b"]),
    }
    outs = [("y_prompt", (SEQ, D)), ("y_sample", (TS, D)), ("new_a_prompt", (HA, D)), ("new_b_prompt", (HB, D)),
            ("new_a_sample", (DEC_B, HA, D)), ("new_b_sample", (DEC_B, HB, D))]
    nc = bacc.Bacc("TRN2", target_bir_lowering=False, num_devices=1)
    aps, feed = [], {}
    for name, a in arrays.items():
        a = np.ascontiguousarray(a)
        feed[f"in_{name}"] = a
        aps.append(nc.dram_tensor(f"in_{name}", a.shape, mybir.dt.from_np(a.dtype), kind="ExternalInput").ap())
    for name, shape in outs:
        aps.append(nc.dram_tensor(f"out_{name}", shape, F32, kind="ExternalOutput").ap())
    hybrid_step(nc, *aps)
    r = run_bass_kernel_spmd(nc, [feed], core_ids=[0]).results[0]
    y_p, y_s, a_p, b_p, a_s, b_s = (r[f"out_{name}"] for name, _ in outs)
    return (y_p.reshape(1, SEQ, D), y_s.reshape(DEC_B, DEC_T, D), a_p.reshape(1, 1, HA, D),
            b_p.reshape(1, 1, HB, D), a_s.reshape(1, DEC_B, HA, D), b_s.reshape(1, DEC_B, HB, D))
```

```python
from contextlib import ExitStack

import concourse.bass as bass
from concourse import mybir

F32 = mybir.dt.float32
F32R = mybir.dt.float32r
U32 = mybir.dt.uint32
ALU = mybir.AluOpType
ACT = mybir.ActivationFunctionType
AX = mybir.AxisListType

P = 128
D = 2048
NCH = D // P
SEQ, DEC_B, DEC_T = 256, 8, 4
TS = DEC_B * DEC_T
N = SEQ + TS
WA, WB = 31, 3
HA, HB = WA - 1, WB - 1
HEADS, NKEYS, TOPK = 8, 128, 16
ALPHA = 2.0 ** 0.25
EPS = 1e-5

GC = 4
NG = NCH // GC
UNITS = 8
RING = 4
NMOD = 6 * NG
NM = 32
NQ = 7
A_GATE, A_VAL, C_GATE, H_IN, B_GATE, GATE_A, GATE_B = 1, 0, 3, 4, 2, 5, 6
ORDER = [A_GATE, A_VAL, C_GATE, H_IN, B_GATE, GATE_A, GATE_B]
NIN = NQ * NG
SH1, SC1, G1, SH2, SC2, G2 = range(6)

R_WA, R_WB, R_BA, R_AG, R_AB, R_1G, R_1B, R_MOD, R_C = 0, 31, 34, 35, 36, 37, 38, 39, 45
NROW = 45 + 1 + DEC_B
NMC = 1 + DEC_B

BLOCKS = [(0, 1, 16), (1, 1, 8), (2, 2, 5), (4, 4, 3), (8, 8, 1)]
NCAND = sum(r * n for _, r, n in BLOCKS)
LOWEST = -3.4e38

TILES = [(0, 7), (8, 9), (10, 17)]
STEPS = 18
SAMPLES = 1
ROWS = [P, TS, P]
SCORE_ROUNDS = [(0, 8), (8, 8), (16, 2)]


def at_least(eng, sem, value):
    if isinstance(value, int):
        if value > 0:
            eng.wait_ge(sem, value)
    else:
        eng.wait_ge(sem, value)


def at_least_apart(eng, sem, value):
    at_least(eng, sem, value)
    if not isinstance(value, int):
        eng.nop(nofuse=True)


class Chain:

    def __init__(self, eng, sem):
        self.eng, self.sem, self.n = eng, sem, 0

    def restart(self):
        self.all()
        self.eng.sem_clear(self.sem)
        self.n = 0

    def link(self, ins):
        ins.then_inc(self.sem, 1)
        self.n += 1
        return self

    def all(self):
        at_least(self.eng, self.sem, self.n)

    def back(self, k):
        at_least(self.eng, self.sem, self.n - k)


def hybrid_step(nc, x_prompt, x_sample, state_a, state_b, c_prompt, c_sample, w_mod, b_mod, w_in,
                conv_a_w, conv_a_b, ln_a_g, ln_a_b, w_a_out, conv_b_w, w_b_out, w_o, ln1_g, ln1_b,
                w_q, sub_keys, peer_u, peer_v, ln2_g, ln2_b,
                y_prompt, y_sample, new_a_prompt, new_b_prompt, new_a_sample, new_b_sample):
    with ExitStack() as ctx:
        base = 16512

        def at(name, offset, shape, dt=F32):
            return nc.alloc_sbuf_tensor_at(name, shape, dt, offset=base + offset)

        def sem(name):
            return ctx.enter_context(nc.semaphore(name))

        R = NCH * N * 4
        xT = at("xT", 0, [P, NCH, N])
        ybT = at("ybT", R, [P, NCH, N])
        actH = at("actH", 2 * R, [P, NCH, N], F32R)
        actL = at("actL", 3 * R, [P, NCH, N], F32R)
        cyT = at("cyT", 4 * R, [P, NCH, N])
        wH = at("wH", 5 * R, [P, RING, 2, 512], F32R)
        wL = at("wL", 5 * R + 16384, [P, RING, 2, 512], F32R)
        sgB = at("sgB", 124928, [P, NCH, N])
        raw = at("raw", 143360, [P, RING, 2, 512])
        sgA = at("sgA", 159744, [P, NCH, N])
        M0 = 178176
        gluP = at("gluP", M0, [P, GC, HA + SEQ])
        gluS = at("gluS", M0 + 4576, [P, GC, DEC_B, HA + DEC_T])
        cbP = at("cbP", M0 + 8928, [P, GC, HB + SEQ])
        cbS = at("cbS", M0 + 13056, [P, GC, DEC_B, HB + DEC_T])
        tmp = at("tmp", M0 + 13824, [P, GC, N])
        acc = at("acc", M0 + 18432, [P, GC, N])
        modT = at("modT", M0 + 23040, [P, 6 * NCH, NMC])
        par = at("par", M0 + 26496, [P, NCH, NROW])
        ident = at("ident", M0 + 29952, [P, P])
        ones = at("ones", M0 + 30464, [P, P])
        siluC = at("siluC", 176128, [P, NCH, NM])
        mean = at("mean", M0 + 31552, [P, N])
        rstd = at("rstd", M0 + 32704, [P, N])
        tail = at("tail", M0 + 31552, [P, GC, 96])
        wAg = at("wAg", M0 + 33856, [P, GC, WA])
        wBg = at("wBg", M0 + 34368, [P, GC, WB + 1])
        sel = at("sel", M0 + 34432, [P, NMC])
        modRing = at("modRing", 5 * R, [P, UNITS, 2, 512])
        modZ = at("modZ", M0 + 13824, [P, 2, 512])
        xRaw = at("xRaw", 159744, [P, 2, D])
        parRaw = at("parRaw", 124928, [NROW, D])
        xsRaw = at("xsRaw", 124928 + 8192, [TS, D])
        stARaw = at("stARaw", R, [4 * HA, 2, D])
        stBRaw = at("stBRaw", 2 * R, [DEC_B * HB, D])
        tails = at("tails", M0 + 13824, [P, NCH, 96])
        modB = at("modB", M0 + 9216, [P, NCH, NMC])
        keyRaw = at("keyRaw", 124928, [P, 2 * HEADS, P])
        sampleM = at("sampleM", M0 + 8192, [P, GC, DEC_B, DEC_T])
        keyT = at("keyT", M0, [P, 2 * HEADS, P])
        outA = at("outA", 124928 + 8192, [HA + TS, D])
        outB = at("outB", 159744, [HB + TS, D])
        fin = at("fin", 0, [P, D])
        g2S = at("g2S", 8192, [TS, D])
        scores = at("scores", 2 * R, [P, STEPS, 2, NKEYS])
        x1Tok = [at("x1Prompt0", 3 * R, [P, D]), at("x1Sample", M0, [TS, D]), at("x1Prompt1", 3 * R + 8192, [P, D])]
        vRing = at("vRing", 4 * R, [P, 4, D])
        g2pRep = at("g2pRep", 106496, [P, NCH, P])
        diag = at("diag", 106496, [P, TOPK, P])
        g2sRep = at("g2sRep", 114688, [P, NCH, TS])
        g2P = at("g2P", 116736, [P, D])
        lnG = at("lnG", 143360, [P, D])
        lnB = at("lnB", 151552, [P, D])
        uRing = [at(f"uRow{k}", o, [P, D]) for k, o in enumerate((124928, 133120, 159744, 167936))]
        T0 = M0 + 13824
        sc0 = at("sc0", T0, [P, 2, NKEYS])
        sc1 = at("sc1", T0 + 1024, [P, 2, NKEYS])
        onehot = at("onehot", T0 + 2048, [P, TOPK, NCAND])
        iota = at("iota", T0 + 5504, [P, NCAND], mybir.dt.int32)
        iotaF = at("iotaF", T0 + 5728, [P, NCAND])
        cand = at("cand", T0 + 5952, [P, NCAND])
        cand2 = at("cand2", T0 + 6176, [P, NCAND])
        candId = at("candId", T0 + 6400, [P, NCAND])
        top = at("top", T0 + 6624, [P, 2, TOPK])
        topIx = at("topIx", T0 + 6752, [P, 2, TOPK], U32)
        topIxF = at("topIxF", T0 + 6880, [P, 2, TOPK])
        pos = at("pos", T0 + 7008, [P, TOPK], U32)
        posF = at("posF", T0 + 7072, [P, TOPK])
        best = at("best", T0 + 7136, [P, 2, TOPK])
        negMax = at("negMax", T0 + 7264, [P, 2])
        eidF = at("eidF", T0 + 7296, [P, TOPK])
        idxU = at("idxU", T0 + 7360, [P, 2, TOPK], U32)
        idxV = at("idxV", T0 + 7488, [P, 2, TOPK], U32)
        dots = at("dots", T0 + 7616, [P, 2, TOPK])
        gel = at("gel", T0 + 7744, [P, TOPK])
        ex = at("ex", T0 + 7808, [P, TOPK])
        exSum = at("exSum", T0 + 7872, [P, 1])
        exInv = at("exInv", T0 + 7904, [P, 1])
        wts = at("wts", T0 + 7936, [P, 2, TOPK])
        fold = at("fold", T0 + 8064, [P, TS])
        stats = at("stats", T0 + 8192, [P, 4, 6])
        mv = at("mv", T0 + 8288, [P, 2])
        ve = at("ve", T0 + 8320, [P, 3])

        ps = ctx.enter_context(nc.psum_tensor("ps", [P, 8, 512], F32))

        tailScratch = nc.dram_tensor("tail_scratch", (P, NCH * 96), F32, kind="Internal").ap()

        loaded_par = sem("loaded_par")
        loaded_x = sem("loaded_x")
        loaded_state = sem("loaded_state")
        const_ready = sem("const_ready")
        pool_chain = sem("pool_chain")
        turned = sem("turned")
        turned_out = sem("turned_out")
        mod_begun = sem("mod_begun")
        mod_in = [sem(f"mod_in{k}") for k in range(UNITS)]
        mod_copied = sem("mod_copied")
        mod_folded = sem("mod_folded")
        raw_in = [sem(f"raw_in{k}") for k in range(RING)]
        hi_ready = sem("hi_ready")
        lo_ready = sem("lo_ready")
        mm_unit = sem("mm_unit")
        mod_unit = sem("mod_unit")
        mod_out = sem("mod_out")
        psum_free = sem("psum_free")
        src_ready = sem("src_ready")
        act_hi = sem("act_hi")
        act_lo = sem("act_lo")
        conv_done = sem("conv_done")
        conv_kept = sem("conv_kept")
        tail_ready = sem("tail_ready")
        tail_saved = sem("tail_saved")
        tail_back = sem("tail_back")
        v_chain = sem("v_chain")
        a_chain = sem("a_chain")
        x_scaled = sem("x_scaled")
        parts_done = sem("parts_done")
        parts_out = sem("parts_out")
        sum_done = sem("sum_done")
        mean_ready = sem("mean_ready")
        centred = sem("centred")
        squared = sem("squared")
        sq_done = sem("sq_done")
        var_ready = sem("var_ready")
        sd_ready = sem("sd_ready")
        normed = sem("normed")
        affine = sem("affine")
        key_in = sem("key_in")
        side_turned = sem("side_turned")
        side_out = sem("side_out")
        new_out = sem("new_out")
        ln_in = sem("ln_in")
        gates_done = sem("gates_done")
        scored = sem("scored")
        scores_out = sem("scores_out")
        rep_ready = sem("rep_ready")
        u2_ready = sem("u2_ready")
        idx_ready = sem("idx_ready")
        idxv_ready = sem("idxv_ready")
        u_in = [sem(f"u_in{k}") for k in range(4)]
        v_in = [sem(f"v_in{k}") for k in range(4)]
        dot_done = sem("dot_done")
        act_done = sem("act_done")
        wts_ready = sem("wts_ready")
        diag_ready = sem("diag_ready")
        v_done = sem("v_done")
        f_free = sem("f_free")
        fs_ready = sem("fs_ready")
        folded = sem("folded")
        ve_ready = sem("ve_ready")
        sdev_ready = sem("sdev_ready")
        y_ready = sem("y_ready")
        y_out = sem("y_out")
        state_out = sem("state_out")

        w_in_v = w_in.rearrange("(k p) n -> p k n", p=P)
        w_mod_v = w_mod.rearrange("(k p) n -> p k n", p=P)
        tails_w = [w.rearrange("(k p) n -> p k n", p=P) for w in (w_b_out, w_a_out, w_o, w_q)]
        AHEAD = 3
        C_OUT = NIN
        block = ctx.enter_context(nc.Block())

        def bank_set(c):
            return 4 * (c % 2) if isinstance(c, int) else (c & 1) * 4

        def group(c, lo=0, hi=N):
            return ps[:, bass.ds(bank_set(c), 4), lo:hi]

        def raw_count(c, u):
            return 16 * (2 * c + u // RING + 1)

        @block.sync
        def _(sp):
            rows = [(conv_a_w, R_WA, WA), (conv_b_w, R_WB, WB), (conv_a_b, R_BA, 1), (ln_a_g, R_AG, 1),
                    (ln_a_b, R_AB, 1), (ln1_g, R_1G, 1), (ln1_b, R_1B, 1), (b_mod, R_MOD, 6),
                    (c_prompt, R_C, 1), (c_sample, R_C + 1, DEC_B)]
            for src, r, n in rows:
                sp.dma_start(parRaw[r:r + n, :], src).then_inc(loaded_par, 16)

            def mod_units(c):
                for u in range(UNITS):
                    at_least_apart(sp, mod_unit, UNITS * (c - 1) + u + 1)
                    sp.dma_start(modRing[:, u], w_mod_v[:, 2 * u:2 * u + 2, bass.ds(c * 512, 512)])\
                      .then_inc(mod_in[u], 16)

            sp.dma_start(xRaw[:, :, :], x_prompt.rearrange("(t p) d -> p t d", p=P)).then_inc(loaded_x, 16)
            sp.dma_start(xsRaw[:, :], x_sample).then_inc(loaded_x, 16)
            mod_units(0)
            mod_units(1)
            sp.dma_start(stARaw[:, :, :], state_a.rearrange("(h q) d -> q h d", h=2)).then_inc(loaded_state, 16)
            sp.dma_start(stBRaw[:, :], state_b).then_inc(loaded_state, 16)
            with sp.Fori(2, NMOD) as c:
                mod_units(c)

            def in_group(g, q):
                c = NQ * g + q
                col = ORDER[q] * D + g * 512
                for u in range(UNITS):
                    at_least_apart(sp, lo_ready, UNITS * c + u - RING + 1)
                    sp.dma_start(raw[:, u % RING], w_in_v[:, 2 * u:2 * u + 2, bass.ds(col, 512)])\
                      .then_inc(raw_in[u % RING], 16)

            for q in range(NQ):
                in_group(0, q)
            with sp.Fori(1, NG) as g:
                for q in range(NQ):
                    in_group(g, q)

            for w, src in enumerate(tails_w):
                def out_group(i):
                    for u in range(UNITS):
                        at_least_apart(sp, lo_ready, UNITS * (C_OUT + NG * w + i) + u - RING + 1)
                        sp.dma_start(raw[:, u % RING], src[:, 2 * u:2 * u + 2, bass.ds(i * 512, 512)])\
                          .then_inc(raw_in[u % RING], 16)

                out_group(0)
                if w == 2:
                    sp.wait_ge(gates_done, 1)
                    sp.dma_start(keyRaw[:, :, :], sub_keys.rearrange("h s n k -> n (h s) k")).then_inc(key_in, 16)
                with sp.Fori(1, NG) as i:
                    out_group(i)
            sp.wait_ge(lo_ready, UNITS * (C_OUT + 4 * NG))
            sp.dma_start(lnG[:, :], ln2_g.broadcast_to((P, D))).then_inc(ln_in, 16)
            sp.dma_start(lnB[:, :], ln2_b.broadcast_to((P, D))).then_inc(ln_in, 16)
            for t in range(3):
                sp.wait_ge(y_ready, t + 1)
                dst = y_sample if t == SAMPLES else y_prompt[t // 2 * P:(t // 2 + 1) * P, :]
                sp.dma_start(dst, fin[0:ROWS[t], :]).then_inc(y_out, 16)
            sp.wait_ge(y_out, 48)

        @block.gpsimd
        def _(pool):
            nc.gpsimd.memset(ident[:, :], 0.0).then_inc(pool_chain, 1)
            pool.wait_ge(pool_chain, 1)
            nc.gpsimd.affine_select(out=ident[:, :], in_=ident[:, :], compare_op=ALU.not_equal, fill=1.0,
                                    base=0, pattern=[[-1, P]], channel_multiplier=1).then_inc(const_ready, 1)
            nc.gpsimd.memset(ones[:, :], 1.0).then_inc(const_ready, 1)
            nc.gpsimd.memset(siluC[:, :, NMC:NM], 0.0).then_inc(const_ready, 1)
            nc.gpsimd.memset(gluP[:, :, 0:HA], 0.0).then_inc(const_ready, 1)
            nc.gpsimd.memset(cbP[:, :, 0:HB], 0.0).then_inc(const_ready, 1)
            with pool.Fori(0, NG) as g:
                at_least_apart(pool, tail_ready, g + 1)
                pool.dma_start(tailScratch[:, bass.ds(g * GC * 96, GC * 96)],
                               tail[:, :, :].rearrange("p a b -> p (a b)")).then_inc(tail_saved, 16)
            pool.dma_start(new_a_sample[:, 0:HA - DEC_T, :],
                           state_a.rearrange("(b r) d -> b r d", r=HA)[:, DEC_T:HA, :]).then_inc(state_out, 16)
            pool.wait_ge(tail_saved, 16 * NG)
            pool.wait_ge(psum_free, NIN)
            pool.wait_ge(conv_kept, NG)
            pool.dma_start(tails[:, :, :].rearrange("p a b -> p (a b)"), tailScratch).then_inc(tail_back, 16)
            pool.wait_ge(side_out, 3)
            pool.dma_start(new_a_prompt, outA[0:HA, :]).then_inc(new_out, 16)
            pool.dma_start(new_a_sample[:, HA - DEC_T:HA, :], outA[HA:HA + TS, :]).then_inc(new_out, 16)
            pool.dma_start(new_b_prompt, outB[0:HB, :]).then_inc(new_out, 16)
            for b in range(DEC_B):
                r = HB + DEC_T * b + DEC_T - HB
                pool.dma_start(new_b_sample[b, :, :], outB[r:r + HB, :]).then_inc(new_out, 16)
            pool.wait_ge(new_out, 16 * (3 + DEC_B))
            nc.gpsimd.iota(iota[:, :], pattern=[[1, NCAND]], base=0, channel_multiplier=0).then_inc(const_ready, 1)

            def gather_u(s, par_, k):
                at_least_apart(pool, dot_done, TOPK * s + k - 3)
                pool.indirect_dma_start(uRing[k % 4][:, :], None, peer_u,
                                        bass.IndirectOffsetOnAxis(ap=idxU[:, par_, k:k + 1], axis=0))\
                    .then_inc(u_in[k % 4], 16)

            def gather_v(s, par_, k):
                at_least_apart(pool, v_done, TOPK * s + k - 3)
                pool.indirect_dma_start(vRing[:, k % 4, :], None, peer_v,
                                        bass.IndirectOffsetOnAxis(ap=idxV[:, par_, k:k + 1], axis=0))\
                    .then_inc(v_in[k % 4], 16)

            def step(s, par_):
                at_least_apart(pool, idx_ready, s + 1)
                for k in range(TOPK):
                    gather_u(s, par_, k)
                    if k == 0:
                        at_least_apart(pool, idxv_ready, s)
                    gather_v(s - 1, 1 - par_, k)

            pool.wait_ge(side_out, 3)
            pool.wait_ge(act_lo, 16)
            pool.wait_ge(idx_ready, 1)
            for k in range(TOPK):
                gather_u(0, 0, k)
            pool.wait_ge(scores_out, 1 + len(SCORE_ROUNDS))
            step(1, 1)
            with pool.Fori(1, STEPS // 2) as i:
                step(2 * i, 0)
                step(2 * i + 1, 1)
            pool.wait_ge(idxv_ready, STEPS)
            for k in range(TOPK):
                gather_v(STEPS - 1, 1, k)
            pool.wait_ge(state_out, 16)

        @block.tensor
        def _(pe):
            pe.wait_ge(const_ready, 5)
            n_turned = [0]

            def turn_round(parts):
                r = n_turned[0]
                at_least(pe, turned_out, r - 1)
                for n in range(GC):
                    for src, at_ in parts(n):
                        k, m = src.shape[0], src.shape[1]
                        last = nc.tensor.transpose(ps[:, 4 * (r % 2) + n, at_:at_ + k], src, ident[0:k, 0:k])
                last.then_inc(turned, 1)
                n_turned[0] += 1

            def cols(g, n):
                return slice((GC * g + n) * P, (GC * g + n + 1) * P)

            pe.wait_ge(loaded_par, 160)
            for g in range(NG):
                turn_round(lambda n: [(parRaw[:, cols(g, n)], 0)])
            pe.wait_ge(loaded_x, 32)
            for g in range(NG):
                turn_round(lambda n: [(xRaw[:, 0, cols(g, n)], 0), (xRaw[:, 1, cols(g, n)], P),
                                      (xsRaw[:, cols(g, n)], SEQ)])
            pe.wait_ge(mod_begun, 10)

            def mod_group(c, par_):
                at_least(pe, mod_copied, c - 1)
                for u in range(UNITS):
                    pe.wait_ge(mod_in[u], 16 * (c + 1))
                    for kk in range(2):
                        kc = 2 * u + kk
                        q = NM * (kc % 4)
                        mm = nc.tensor.matmul(ps[q:q + NM, 4 * par_, :], siluC[:, kc, :], modRing[:, u, kk, :],
                                              start=(kc < 4), stop=(kc >= NCH - 4), skip_group_check=True)
                    mm.then_inc(mod_unit, 1)

            def mod_fold(c, par_):
                pe.wait_ge(mod_copied, c + 1)
                at_least(pe, mod_out, c - 1)
                for n in range(GC):
                    mm = nc.tensor.matmul(ps[:, 4 * par_ + 1, NMC * n:NMC * (n + 1)],
                                          modZ[:, par_, n * P:(n + 1) * P], sel[:, :], start=True, stop=True)
                mm.then_inc(mod_folded, 1)

            pe.wait_ge(turned_out, 8)
            mod_group(0, 0)
            mod_group(1, 1)
            mod_fold(0, 0)
            mod_fold(1, 1)
            pe.wait_ge(mod_out, 2)
            pe.wait_ge(loaded_state, 32)
            for g in range(NG):
                turn_round(lambda n: [(stARaw[:, 0, cols(g, n)], 0), (stARaw[:, 1, cols(g, n)], 4 * HA),
                                      (stBRaw[:, cols(g, n)], 8 * HA)])
            pe.wait_ge(turned_out, 12)
            mod_group(2, 0)
            with pe.Fori(1, NMOD // 2 - 1) as i:
                mod_group(2 * i + 1, 1)
                mod_fold(2 * i, 0)
                mod_group(2 * i + 2, 0)
                mod_fold(2 * i + 1, 1)
            mod_group(NMOD - 1, 1)
            mod_fold(NMOD - 2, 0)
            mod_fold(NMOD - 1, 1)
            pe.wait_ge(mod_out, NMOD)

            def weight_unit(c, par_, u):
                pe.wait_ge(lo_ready, UNITS * c + u + 1)
                for n in range(GC):
                    out = ps[:, 4 * par_ + n, 0:N]
                    for kk in range(2):
                        kc = 2 * u + kk
                        wh = wH[:, u % RING, kk, n * P:(n + 1) * P]
                        wl = wL[:, u % RING, kk, n * P:(n + 1) * P]
                        nc.tensor.matmul(out, wh, actH[:, kc, :], start=(kc == 0), stop=False,
                                         skip_group_check=True)
                        nc.tensor.matmul(out, wh, actL[:, kc, :], start=False, stop=False,
                                         skip_group_check=True)
                        mm = nc.tensor.matmul(out, wl, actH[:, kc, :], start=False, stop=(kc == NCH - 1),
                                              skip_group_check=True)
                mm.then_inc(mm_unit, 1)

            def in_group(c, par_):
                at_least(pe, psum_free, c - 1)
                for u in range(UNITS):
                    if isinstance(c, int) and c == 0 and u % 2 == 0:
                        pe.wait_ge(act_lo, u // 2 + 1)
                    weight_unit(c, par_, u)

            in_group(0, 0)
            in_group(1, 1)
            with pe.Fori(1, NIN // 2) as i:
                in_group(2 * i, 0)
                in_group(2 * i + 1, 1)

            def channel_sum(src, bank, ready, count, quarters=range(NG)):
                for g in quarters:
                    pe.wait_ge(ready, count + g + 1)
                    for n in range(GC):
                        mm = nc.tensor.matmul(ps[NM * n:NM * (n + 1), bank, 0:N], ones[:, 0:NM],
                                              src[:, GC * g + n, :], start=(g == 0), stop=(g == NG - 1),
                                              skip_group_check=True)
                if NG - 1 in quarters:
                    mm.then_inc(parts_done, 1)

            def fold_sum(n, bank, parts, done):
                pe.wait_ge(parts_out, n)
                nc.tensor.matmul(ps[:, bank, 0:N], ones[:, :], parts[:, :], start=True, stop=True).then_inc(done, 1)

            def product(w, hooks=None):
                def out_group(i, par_):
                    c = C_OUT + NG * w + i
                    pe.wait_ge(psum_free, c - 1)
                    for u in range(UNITS):
                        if u % 2 == 0:
                            pe.wait_ge(act_lo, 4 * (w + 1) + u // 2 + 1)
                        if hooks and (i, u) in hooks:
                            hooks[i, u]()
                        weight_unit(c, par_, u)
                if hooks:
                    for i in range(NG):
                        out_group(i, i % 2)
                else:
                    with pe.Fori(0, NG // 2) as i:
                        out_group(2 * i, 0)
                        out_group(2 * i + 1, 1)

            def side(jobs, m, bank):
                for c in range(NCH):
                    last = nc.tensor.transpose(ps[0:m, bank + c // GC, (c % GC) * P:(c % GC + 1) * P],
                                               jobs(c), ident[:, :])
                last.then_inc(side_turned, 1)

            pe.wait_ge(psum_free, NIN)
            channel_sum(cyT, 4, conv_kept, 0)

            def square_sum():
                pe.wait_ge(psum_free, C_OUT + 2)
                channel_sum(ybT, 4, squared, 0)

            product(0, {(0, 2): lambda: fold_sum(1, 4, mean, sum_done),
                        (1, 0): lambda: pe.wait_ge(mean_ready, 1),
                        (2, 3): square_sum,
                        (2, 5): lambda: fold_sum(2, 4, rstd, sq_done),
                        (3, 0): lambda: pe.wait_ge(var_ready, 1)})
            product(1)

            def turn_keys():
                pe.wait_ge(psum_free, C_OUT + 2 * NG + 1)
                pe.wait_ge(key_in, 16)
                side(lambda c: keyRaw[:, c, :], P, 0)

            def turn_tails_a():
                pe.wait_ge(psum_free, C_OUT + 2 * NG + 2)
                pe.wait_ge(tail_back, 16)
                side(lambda c: tails[:, c, 0:HA + TS], HA + TS, 4)

            def turn_tails_b():
                pe.wait_ge(psum_free, C_OUT + 2 * NG + 3)
                side(lambda c: tails[:, c, HA + TS:96], HB + TS, 0)

            def first_sums():
                pe.wait_ge(side_out, 3)
                channel_sum(xT, 0, psum_free, C_OUT + 2 * NG, range(NG - 1))

            product(2, {(1, 5): turn_keys, (2, 0): lambda: pe.wait_ge(side_out, 1),
                        (2, 5): turn_tails_a, (3, 0): lambda: pe.wait_ge(side_out, 2),
                        (3, 4): turn_tails_b, (3, 7): first_sums})
            channel_sum(xT, 0, psum_free, C_OUT + 2 * NG, [NG - 1])
            fold_sum(3, 0, mean, sum_done)
            channel_sum(ybT, 1, squared, 4)
            fold_sum(4, 1, rstd, sq_done)
            pe.wait_ge(var_ready, 2)
            def score(s, bank):
                at_ = (s % 2) * 2 * NKEYS
                for side_ in range(2):
                    o = at_ + side_ * NKEYS
                    if TILES[SAMPLES][0] <= s <= TILES[SAMPLES][1]:
                        for r in range(4):
                            hs = 2 * (2 * r + s - TILES[SAMPLES][0]) + side_
                            mm = nc.tensor.matmul(ps[32 * r:32 * r + TS, bank, o:o + NKEYS], cyT[:, hs, SEQ:N],
                                                  keyT[:, hs, :], start=True, stop=True)
                    else:
                        t, h = (0, s) if s < HEADS else (1, s - TILES[2][0])
                        hs = 2 * h + side_
                        mm = nc.tensor.matmul(ps[:, bank, o:o + NKEYS], cyT[:, hs, t * P:(t + 1) * P],
                                              keyT[:, hs, :], start=True, stop=True)
                return mm

            def first_scores():
                pe.wait_ge(psum_free, C_OUT + 3 * NG + 1)
                score(0, 0).then_inc(scored, 1)

            product(3, {(1, 5): first_scores, (2, 0): lambda: pe.wait_ge(scores_out, 1)})
            pe.wait_ge(psum_free, C_OUT + 4 * NG)

            def turn_u2(t):
                for c in range(NCH):
                    src = ybT[:, c, 0:P] if t <= SAMPLES else ybT[:, c, P:2 * P]
                    last = nc.tensor.transpose(ps[:, c // GC, (c % GC) * P:(c % GC + 1) * P], src, ident[:, :])
                last.then_inc(u2_ready, 1)

            turn_u2(0)

            for rnd, (first, count) in enumerate(SCORE_ROUNDS):
                pe.wait_ge(scores_out, rnd + 1)
                for s in range(first, first + count):
                    mm = score(s, 4 + (s - first) // 2)
                mm.then_inc(scored, 1)
            pe.wait_ge(scores_out, 1 + len(SCORE_ROUNDS))
            pe.wait_ge(affine, 3 * NCH)
            jobs = [(lambda c: xT[:, c, SEQ:N], TS), (lambda c: xT[:, c, 0:P], P),
                    (lambda c: xT[:, c, P:2 * P], P), (lambda c: g2pRep[:, c, :], P),
                    (lambda c: g2sRep[:, c, :], TS)]
            for n, (job, m) in enumerate(jobs):
                pe.wait_ge(side_out, 3 + n)
                if n == 3:
                    pe.wait_ge(rep_ready, 2)
                side(job, m, 4)
            pe.wait_ge(side_out, 8)

            def add_experts(s, first):
                for k in range(TOPK):
                    pe.wait_ge(diag_ready, TOPK * s + k + 1)
                    pe.wait_ge(v_in[k % 4], 16 * (4 * s + k // 4 + 1))
                    for n in range(4):
                        mm = nc.tensor.matmul(ps[:, 4 + n, :], diag[:, k, :], vRing[:, k % 4, n * 512:(n + 1) * 512],
                                              start=(first and k == 0), stop=True, skip_group_check=True)
                    mm.then_inc(v_done, 1)

            for t, (a, b) in enumerate(TILES):
                if t == SAMPLES + 1:
                    pe.wait_ge(fs_ready, 1)
                    for n in range(4):
                        mm = nc.tensor.matmul(ps[0:TS, 4 + n, :], fold[:, :], fin[:, n * 512:(n + 1) * 512],
                                              start=True, stop=True)
                    mm.then_inc(folded, 1)
                at_least(pe, f_free, t)
                add_experts(a, True)
                if b - a > 1:
                    with pe.Fori(a + 1, b) as s:
                        add_experts(s, False)
                if t < 2:
                    pe.wait_ge(dot_done, TOPK * (b + 1))
                    if t + 1 == SAMPLES:
                        pe.wait_ge(rep_ready, 3)
                    turn_u2(t + 1)
                add_experts(b, False)

        @block.scalar
        def _(act):
            chain = Chain(act, a_chain)
            act.wait_ge(turned_out, 4)
            act.wait_ge(const_ready, 5)
            nc.scalar.activation(siluC[:, :, 0:NMC], par[:, :, R_C:R_C + NMC], ACT.Silu).then_inc(mod_begun, 1)

            def split_part(k, src):
                nc.scalar.activation(actH[:, GC * k:GC * k + GC, :], src[:, GC * k:GC * k + GC, :],
                                     ACT.Copy).then_inc(act_hi, 1)

            def weights(c, u):
                act.wait_ge(raw_in[u % RING], raw_count(c, u))
                at_least_apart(act, mm_unit, UNITS * c + u - RING + 1)
                nc.scalar.activation(wH[:, u % RING], raw[:, u % RING], ACT.Copy).then_inc(hi_ready, 1)

            def mod_copy(c, par_):
                at_least(act, mod_folded, c - 1)
                at_least_apart(act, mod_unit, UNITS * (c + 1))
                nc.scalar.activation(modZ[:, par_, :], ps[:, 4 * par_, :], ACT.Copy).then_inc(mod_copied, 1)

            FIRST = 2 * NG
            mod_copy(0, 0)
            mod_copy(1, 1)
            with act.Fori(1, FIRST // 2) as i:
                mod_copy(2 * i, 0)
                mod_copy(2 * i + 1, 1)
            for k in range(4):
                mod_copy(FIRST + k, k % 2)
                act.wait_ge(src_ready, k + 1)
                split_part(k, ybT)
            nc.scalar.activation(xT[:, :, :], xT[:, :, :], ACT.Copy, scale=ALPHA).then_inc(x_scaled, 1)
            with act.Fori(FIRST // 2 + 2, NMOD // 2) as i:
                mod_copy(2 * i, 0)
                mod_copy(2 * i + 1, 1)
            act.wait_ge(mod_unit, UNITS * NMOD)

            def evacuate(g, q):
                c = NQ * g + q
                if ORDER[q] in (A_VAL, H_IN, B_GATE):
                    return
                act.wait_ge(mm_unit, UNITS * (c + 1))
                at_least_apart(act, psum_free, c)
                if ORDER[q] == A_GATE:
                    out, f = tmp[:, :, :], ACT.Sigmoid
                elif ORDER[q] == C_GATE:
                    out, f = tmp[:, :, :], ACT.Copy
                else:
                    gate = sgA if ORDER[q] == GATE_A else sgB
                    out, f = gate[:, bass.ds(g * GC, GC), :], ACT.Sigmoid
                nc.scalar.activation(out, group(c), f).then_inc(psum_free, 1)

            def keep_conv(g):
                at_least_apart(act, conv_done, g + 1)
                nc.scalar.activation(cyT[:, bass.ds(g * GC, GC), :], acc[:, :, :], ACT.Copy).then_inc(conv_kept, 1)

            def in_groups(g, first):
                for q in range(NQ):
                    c = NQ * g + q
                    for u in range(UNITS):
                        if u == 3:
                            if q > 0:
                                evacuate(g, q - 1)
                            elif not first:
                                evacuate(g - 1, NQ - 1)
                        weights(c, u)
                        if q == 2 and u == 2 and not first:
                            keep_conv(g - 1)
                        if q == 5 and u == 5:
                            if not first:
                                at_least_apart(act, tail_saved, 16 * g)
                            at_least_apart(act, psum_free, NQ * g + 4)
                            chain.restart()
                            for at_, src in ((0, gluP[:, :, SEQ:SEQ + HA]), (HA + TS, cbP[:, :, SEQ:SEQ + HB])):
                                chain.link(nc.scalar.activation(tail[:, :, at_:at_ + src.shape[2]], src, ACT.Copy))
                            chain.link(nc.scalar.activation(
                                tail[:, :, HA:HA + TS].rearrange("p n (b t) -> p n b t", b=DEC_B),
                                gluS[:, :, :, HA:HA + DEC_T], ACT.Copy))
                            chain.all()
                            nc.scalar.activation(
                                tail[:, :, 96 - TS:96].rearrange("p n (b t) -> p n b t", b=DEC_B),
                                cbS[:, :, :, HB:HB + DEC_T], ACT.Copy).then_inc(tail_ready, 1)

            in_groups(0, True)
            with act.Fori(1, NG) as g:
                in_groups(g, False)
            keep_conv(NG - 1)

            def weights_ahead(w):
                for u in range(AHEAD):
                    weights(C_OUT + NG * w, u)

            def product(w, hooks=None, evac=None):
                def out_group(i):
                    for u in range(UNITS):
                        if not (isinstance(i, int) and i == 0 and u < AHEAD):
                            weights(C_OUT + NG * w + i, u)
                        if hooks and (i, u) in hooks:
                            hooks[i, u]()
                        if u == 3 and evac and not (isinstance(i, int) and i == 0):
                            evac(i - 1)
                for i in range(NG if hooks else 1):
                    out_group(i)
                if not hooks:
                    with act.Fori(1, NG) as i:
                        out_group(i)
                if evac:
                    evac(NG - 1)

            def parts_copy(n, out, bank):
                act.wait_ge(parts_done, n)
                nc.scalar.activation(out[:, :], ps[:, bank, 0:N], ACT.Copy).then_inc(parts_out, 1)

            def take_mean(n, bank):
                act.wait_ge(sum_done, n)
                nc.scalar.activation(mean[:, :], ps[:, bank, 0:N], ACT.Copy, scale=1.0 / (NM * D))\
                  .then_inc(mean_ready, 1)

            def square(src, n, k):
                act.wait_ge(centred, 4 * n + k + 1)
                nc.scalar.activation(ybT[:, GC * k:GC * k + GC, :], src[:, GC * k:GC * k + GC, :],
                                     ACT.Square).then_inc(squared, 1)

            def deviation(n):
                act.wait_ge(var_ready, n + 1)
                nc.scalar.activation(rstd[:, :], rstd[:, :], ACT.Sqrt).then_inc(sd_ready, 1)

            def apply(src, k, f, rg, rb):
                for c in range(GC * k, GC * k + GC):
                    nc.scalar.activation(src[:, c, :], src[:, c, :], f, scale=par[:, c, rg:rg + 1],
                                         bias=par[:, c, rb:rb + 1]).then_inc(affine, 1)

            weights_ahead(0)
            act.wait_ge(src_ready, 8)
            act.wait_ge(mm_unit, UNITS * NIN)
            split_part(0, ybT)
            evacuate(NG - 1, NQ - 1)
            for k in range(1, 4):
                split_part(k, ybT)
            act.wait_ge(tail_saved, 16 * NG)
            parts_copy(1, mean, 4)

            def square_a(k):
                act.wait_ge(act_lo, 8)
                square(cyT, 0, k)

            def silu_a(k):
                act.wait_ge(normed, k + 1)
                apply(cyT, k, ACT.Silu, R_AG, R_AB)

            product(0, {(0, 5): lambda: take_mean(1, 4),
                        (1, 0): lambda: square_a(0), (1, 1): lambda: square_a(1),
                        (1, 2): lambda: square_a(2), (1, 3): lambda: square_a(3),
                        (2, 6): lambda: parts_copy(2, rstd, 4), (3, 0): lambda: deviation(0),
                        (3, 3): lambda: silu_a(0), (3, 4): lambda: silu_a(1),
                        (3, 5): lambda: silu_a(2), (3, 6): lambda: silu_a(3)})

            def split_after(src, ready, counts, mm):
                act.wait_ge(mm_unit, mm)
                for k in range(4):
                    act.wait_ge(ready, counts[k])
                    split_part(k, src)

            weights_ahead(1)
            split_after(cyT, affine, [4, 8, 12, 16], UNITS * (C_OUT + NG))
            product(1)
            weights_ahead(2)
            split_after(sgA, psum_free, [C_OUT + NG + k + 1 for k in range(4)], UNITS * (C_OUT + 2 * NG))

            def rows(t):
                return t.rearrange("p (b n) -> p b n", b=4)

            def side_copy(n, out, src, scale=1.0):
                act.wait_ge(side_turned, n)
                nc.scalar.activation(out, src, ACT.Copy, scale=scale).then_inc(side_out, 1)

            def tails_b():
                act.wait_ge(act_lo, 16)
                side_copy(3, rows(outB[:, :]), ps[0:HB + TS, 0:4, :])

            product(2, {(2, 1): lambda: side_copy(1, keyT[:, :, :].rearrange("p (b a) k -> p b (a k)", b=4),
                                                  ps[:, 0:4, :]),
                        (3, 1): lambda: side_copy(2, rows(outA[:, :]), ps[0:HA + TS, 4:8, :]),
                        (3, 7): tails_b})
            weights_ahead(3)
            parts_copy(3, mean, 0)
            take_mean(2, 0)
            for k in range(4):
                square(xT, 1, k)
            parts_copy(4, rstd, 1)
            deviation(1)
            for k in range(4):
                act.wait_ge(normed, 4 + k + 1)
                for c in range(GC * k, GC * k + GC):
                    nc.scalar.activation(ybT[:, c, 0:SEQ], xT[:, c, 0:SEQ], ACT.Identity,
                                         scale=modT[:, SC2 * NCH + c, 0:1], bias=modT[:, SH2 * NCH + c, 0:1])\
                      .then_inc(affine, 1)
                act.wait_ge(affine, NCH + GC * (k + 1))
                act.wait_ge(src_ready, 8 + k + 1)
                split_part(k, ybT)

            def queries(i):
                c = C_OUT + 3 * NG + i
                act.wait_ge(mm_unit, UNITS * (c + 1))
                at_least_apart(act, psum_free, c)
                nc.scalar.activation(cyT[:, bass.ds(i * GC, GC), :], group(c), ACT.Copy).then_inc(psum_free, 1)

            def first_scores():
                act.wait_ge(scored, 1)
                nc.scalar.activation(sc0[:, :, :].rearrange("p s k -> p (s k)"), ps[:, 0, 0:2 * NKEYS],
                                     ACT.Copy).then_inc(scores_out, 1)

            product(3, {(0, 3): lambda: apply(xT, 0, ACT.Identity, R_1G, R_1B),
                        (0, 4): lambda: apply(xT, 1, ACT.Identity, R_1G, R_1B),
                        (0, 5): lambda: apply(xT, 2, ACT.Identity, R_1G, R_1B),
                        (0, 6): lambda: apply(xT, 3, ACT.Identity, R_1G, R_1B),
                        (2, 0): first_scores}, queries)

            for rnd, (first, count) in enumerate(SCORE_ROUNDS):
                act.wait_ge(scored, rnd + 2)
                nc.scalar.activation(
                    scores[:, first:first + count].rearrange("p (b e) s k -> p b (e s k)", e=2),
                    ps[:, 4:4 + count // 2, :], ACT.Copy).then_inc(scores_out, 1)
            nc.scalar.activation(g2pRep[:, :, :], modT[:, G2 * NCH:(G2 + 1) * NCH, 0:1].broadcast_to((P, NCH, P)),
                                 ACT.Copy).then_inc(rep_ready, 1)
            for b in range(DEC_B):
                a = nc.scalar.activation(
                    g2sRep[:, :, DEC_T * b:DEC_T * b + DEC_T],
                    modT[:, G2 * NCH:(G2 + 1) * NCH, 1 + b:2 + b].broadcast_to((P, NCH, DEC_T)), ACT.Copy)
                if b < DEC_B - 1:
                    chain.link(a)
            chain.all()
            a.then_inc(rep_ready, 1)

            side_copy(4, rows(x1Tok[SAMPLES][:, :]), ps[0:TS, 4:8, :], ALPHA)
            side_copy(5, rows(x1Tok[0][:, :]), ps[:, 4:8, :], ALPHA)
            side_copy(6, rows(x1Tok[2][:, :]), ps[:, 4:8, :], ALPHA)
            side_copy(7, rows(g2P[:, :]), ps[:, 4:8, :])
            side_copy(8, rows(g2S[:, :]), ps[0:TS, 4:8, :])
            act.wait_ge(u2_ready, 1)
            for r in range(4):
                a = nc.scalar.activation(ybT[:, :, TS * r:TS * r + TS], ybT[:, :, SEQ:N], ACT.Copy)
                if r < 3:
                    chain.link(a)
            chain.all()
            a.then_inc(rep_ready, 1)

            def step(s, par_, first=False):
                at_least_apart(act, dot_done, TOPK * (s + 1))
                nc.scalar.activation(gel[:, :], dots[:, par_, :], ACT.Gelu).then_inc(act_done, 1)
                nc.scalar.activation(ex[:, :], best[:, par_, :], ACT.Exp, bias=negMax[:, par_:par_ + 1],
                                     accum_out=exSum[:, :]).then_inc(act_done, 1)
                at_least_apart(act, wts_ready, s + 1)
                for k in range(TOPK):
                    if not first:
                        at_least_apart(act, v_done, TOPK * (s - 1) + k + 1)
                    nc.scalar.activation(diag[:, k, :], ident[:, :], ACT.Copy,
                                         scale=wts[:, par_, k:k + 1]).then_inc(diag_ready, 1)

            def deviation2(t):
                act.wait_ge(ve_ready, t + 1)
                m = ROWS[t]
                nc.scalar.activation(ve[0:m, 1:2], ve[0:m, 0:1], ACT.Sqrt).then_inc(sdev_ready, 1)

            act.wait_ge(side_turned, 7)
            for t, (a, b) in enumerate(TILES):
                step(a, 0, t == 0)
                if t > 0:
                    deviation2(t - 1)
                step(a + 1, 1)
                if b - a > 1:
                    with act.Fori(0, (b - a - 1) // 2) as i:
                        step(a + 2 + 2 * i, 0)
                        step(a + 3 + 2 * i, 1)
            deviation2(2)

        @block.vector
        def _(dve):
            chain = Chain(dve, v_chain)
            V = nc.vector

            def copy_round(r, outs):
                dve.wait_ge(turned, r + 1)
                for n, (out, src) in enumerate(outs):
                    i = V.tensor_copy(out, src)
                    if n < len(outs) - 1:
                        chain.link(i)
                        chain.all()
                i.then_inc(turned_out, 1)

            def bset(r):
                return slice(4 * (r % 2), 4 * (r % 2) + 4)

            for g in range(NG):
                copy_round(g, [(par[:, GC * g:GC * g + GC, :], ps[:, bset(g), 0:NROW])])
            dve.wait_ge(turned_out, 4)
            for s in range(6):
                V.tensor_scalar(modT[:, s * NCH:(s + 1) * NCH, :],
                                par[:, :, R_MOD + s:R_MOD + s + 1].broadcast_to((P, NCH, NMC)),
                                1.0 if s in (SC1, G1, SC2, G2) else 0.0, None, ALU.add).then_inc(mod_begun, 1)
            V.tensor_tensor(sel[:, :], ident[:, 0:NMC], ident[:, NM:NM + NMC], ALU.add).then_inc(mod_begun, 1)
            for r in range(2, 4):
                dve.wait_ge(mod_begun, 6 + r)
                V.tensor_tensor(sel[:, :], sel[:, :], ident[:, NM * r:NM * r + NMC], ALU.add).then_inc(mod_begun, 1)
            dve.wait_ge(mod_begun, 10)
            for g in range(NG):
                copy_round(4 + g, [(xT[:, GC * g:GC * g + GC, :], ps[:, bset(g), 0:N])])

            def pre_mod(c, par_):
                at_least_apart(dve, mod_folded, c + 1)
                at_ = modT[:, bass.ds(c * GC, GC), :]
                src = ps[:, 4 * par_ + 1, 0:GC * NMC].rearrange("p (n r) -> p n r", n=GC)
                V.tensor_tensor(at_, at_, src, ALU.add).then_inc(mod_out, 1)

            pre_mod(0, 0)
            pre_mod(1, 1)
            cyA = cyT[:, :, :].rearrange("p (g n) t -> p g (n t)", g=NG)
            for g in range(NG):
                copy_round(8 + g, [
                    (cyA[:, g, 0:GC * 8 * HA].rearrange("p (n t) -> p n t", n=GC), ps[:, bset(g), 0:8 * HA]),
                    (cyA[:, g, GC * 8 * HA:GC * 8 * (HA + HB)].rearrange("p (n t) -> p n t", n=GC),
                     ps[:, bset(g), 8 * HA:8 * (HA + HB)])])
            with dve.Fori(1, NG) as i:
                pre_mod(2 * i, 0)
                pre_mod(2 * i + 1, 1)

            def tokens4(t):
                return t.rearrange("p c (b t) -> p c b t", b=DEC_B)

            def modulate(k, src, sh, sc):
                c0, c1 = sc * NCH, sh * NCH
                part = slice(GC * k, GC * k + GC)
                for c in range(GC * k, GC * k + GC):
                    chain.link(V.tensor_scalar(ybT[:, c, 0:SEQ], src[:, c, 0:SEQ], modT[:, c0 + c, 0:1],
                                               modT[:, c1 + c, 0:1], ALU.mult, ALU.add))
                by = modT[:, c0 + GC * k:c0 + GC * k + GC, 1:NMC].unsqueeze(3).broadcast_to((P, GC, DEC_B, DEC_T))
                off = modT[:, c1 + GC * k:c1 + GC * k + GC, 1:NMC].unsqueeze(3).broadcast_to((P, GC, DEC_B, DEC_T))
                out = tokens4(ybT[:, part, SEQ:N])
                chain.link(V.tensor_tensor(out, tokens4(src[:, part, SEQ:N]), by, ALU.mult))
                chain.all()
                V.tensor_tensor(out, out, off, ALU.add).then_inc(src_ready, 1)

            def split_low_part(n, k, src):
                part = slice(GC * k, GC * k + GC)
                dve.wait_ge(act_hi, 4 * n + k + 1)
                V.tensor_tensor(actL[:, part, :], src[:, part, :], actH[:, part, :].bitcast(F32),
                                ALU.subtract).then_inc(act_lo, 1)

            def split_low(n, src):
                for k in range(4):
                    split_low_part(n, k, src)

            dve.wait_ge(turned_out, 12)
            dve.wait_ge(mod_out, 2 * NG)
            for k in range(4):
                modulate(k, xT, SH1, SC1)
                pre_mod(2 * NG + k, k % 2)
                split_low_part(0, k, ybT)
            with dve.Fori(NG + 2, NMOD // 2) as i:
                pre_mod(2 * i, 0)
                pre_mod(2 * i + 1, 1)

            def weights(c, u):
                at_least_apart(dve, hi_ready, UNITS * c + u + 1)
                V.tensor_tensor(wL[:, u % RING], raw[:, u % RING], wH[:, u % RING].bitcast(F32),
                                ALU.subtract).then_inc(lo_ready, 1)

            def evacuate(g, q):
                c = NQ * g + q
                if ORDER[q] not in (A_VAL, H_IN, B_GATE):
                    return
                at_least_apart(dve, mm_unit, UNITS * (c + 1))
                at_least_apart(dve, psum_free, c)
                if ORDER[q] == B_GATE:
                    V.tensor_tensor(ybT[:, bass.ds(g * GC, GC), :], group(c), tmp[:, :, :], ALU.mult)\
                     .then_inc(psum_free, 1)
                    at_least_apart(dve, psum_free, c + 1)
                    return
                toP, toS, h = (gluP, gluS, HA) if ORDER[q] == A_VAL else (cbP, cbS, HB)
                chain.link(V.tensor_tensor(toP[:, :, h:h + SEQ], group(c, 0, SEQ), tmp[:, :, 0:SEQ], ALU.mult))
                chain.all()
                for n in range(GC):
                    i = V.tensor_tensor(toS[:, n, :, h:h + DEC_T],
                                        ps[:, bass.ds(bank_set(c) + n, 1), SEQ:N].rearrange("p a (b t) -> p (a b) t", b=DEC_B),
                                        tmp[:, n, SEQ:N].rearrange("p (b t) -> p b t", b=DEC_B), ALU.mult)
                    if n < GC - 1:
                        chain.link(i)
                        chain.all()
                i.then_inc(psum_free, 1)
                at_least_apart(dve, psum_free, c + 1)

            def s4(t):
                return t.rearrange("p (b t) -> p b t", b=DEC_B)

            def conv_tap(j):
                for n in range(GC):
                    for lo, out, src in ((0, acc[:, n, 0:SEQ], gluP[:, n, j:j + SEQ]),
                                         (1, s4(acc[:, n, SEQ:N]), gluS[:, n, :, j:j + DEC_T])):
                        w = wAg[:, n, j:j + 1]
                        if j == 0:
                            chain.link(V.tensor_scalar(out, src, w, wBg[:, n, WB:WB + 1], ALU.mult, ALU.add))
                        else:
                            chain.back(2 * GC - 1)
                            chain.link(V.scalar_tensor_tensor(out=out, in0=src, scalar=w, in1=out,
                                                              op0=ALU.mult, op1=ALU.add))

            def conv_b():
                for j in range(WB):
                    for n in range(GC):
                        for out, src in ((tmp[:, n, 0:SEQ], cbP[:, n, j:j + SEQ]),
                                         (s4(tmp[:, n, SEQ:N]), cbS[:, n, :, j:j + DEC_T])):
                            w = wBg[:, n, j:j + 1]
                            if j == 0:
                                chain.link(V.tensor_scalar(out, src, w, None, ALU.mult))
                            else:
                                chain.back(2 * GC - 1)
                                chain.link(V.scalar_tensor_tensor(out=out, in0=src, scalar=w, in1=out,
                                                                  op0=ALU.mult, op1=ALU.add))
                chain.all()

            def begin_group(g, first):
                if not first:
                    at_least_apart(dve, tail_ready, g)
                one = cyA[:, bass.ds(g, 1), :]
                for n in range(GC):
                    chain.link(V.tensor_copy(
                        gluS[:, n, :, 0:HA],
                        one[:, :, n * 8 * HA:(n + 1) * 8 * HA].rearrange("p g (b r) -> p (g b) r", b=DEC_B)))
                    chain.link(V.tensor_copy(
                        cbS[:, n, :, 0:HB],
                        one[:, :, GC * 8 * HA + n * 8 * HB:GC * 8 * HA + (n + 1) * 8 * HB]
                        .rearrange("p g (b r) -> p (g b) r", b=DEC_B)))
                chain.link(V.tensor_copy(wAg[:, :, :], par[:, bass.ds(g * GC, GC), R_WA:R_WA + WA]))
                chain.link(V.tensor_copy(wBg[:, :, :], par[:, bass.ds(g * GC, GC), R_WB:R_WB + WB + 1]))
                chain.all()

            OWN, LATE = 23, 8
            own_units = [(q, u) for q in range(2, NQ) for u in range(UNITS)
                         if (q > 2 or u >= 4) and (q, u) != (4, 4)]
            late_units = [(q, u) for q in (0, 1) for u in range(1, UNITS, 2)]
            spread = {qu for n, qu in enumerate(own_units)
                      if (n + 1) * OWN // len(own_units) > n * OWN // len(own_units)}

            def taps_done():
                chain.all()
                dve.nop(nofuse=True).then_inc(conv_done, 1)

            def in_groups(g, first=False, last=False):
                tap = 0
                for q in range(NQ):
                    c = NQ * g + q
                    for u in range(UNITS):
                        if u == 3 and q > 0:
                            evacuate(g, q - 1)
                        weights(c, u)
                        if (q, u) in late_units and not first:
                            n = late_units.index((q, u))
                            conv_tap(OWN + n)
                            if n == LATE - 1:
                                taps_done()
                        if q == 2 and u == 1:
                            begin_group(g, first)
                        if q == 4 and u == 4:
                            conv_b()
                        if (q, u) in (own_units if last else spread) and tap < WA:
                            if tap == 0 and not first:
                                at_least_apart(dve, conv_kept, g)
                            conv_tap(tap)
                            tap += 1
                            if tap == WA:
                                taps_done()
                chain.restart()

            dve.wait_ge(x_scaled, 1)
            in_groups(0, first=True)
            with dve.Fori(1, NG - 1) as g:
                in_groups(g)
            in_groups(NG - 1, last=True)

            def weights_ahead(w):
                for u in range(AHEAD):
                    weights(C_OUT + NG * w, u)

            def product(w, evac, hooks=None):
                def out_group(i):
                    chain.restart()
                    for u in range(UNITS):
                        if not (isinstance(i, int) and i == 0 and u < AHEAD):
                            weights(C_OUT + NG * w + i, u)
                        if hooks and (i, u) in hooks:
                            hooks[i, u]()
                        if u == 3 and not (isinstance(i, int) and i == 0):
                            evac(i - 1)
                    chain.all()
                if hooks:
                    for i in range(NG):
                        out_group(i)
                else:
                    out_group(0)
                    with dve.Fori(1, NG) as i:
                        out_group(i)
                chain.restart()

            def ready(c):
                at_least_apart(dve, mm_unit, UNITS * (c + 1))
                at_least_apart(dve, psum_free, c)

            def centre(src, n, k):
                if k == 0:
                    dve.wait_ge(mean_ready, n + 1)
                part = src[:, GC * k:GC * k + GC, :]
                V.tensor_tensor(part, part, mean[:, :].unsqueeze(1).broadcast_to((P, GC, N)),
                                ALU.subtract).then_inc(centred, 1)

            def variance(n, bank):
                dve.wait_ge(sq_done, n + 1)
                V.tensor_scalar(rstd[:, :], ps[:, bank, 0:N], 1.0 / (NM * D), EPS, ALU.mult, ALU.add)\
                 .then_inc(var_ready, 1)

            def invert(n):
                dve.wait_ge(sd_ready, n + 1)
                chain.link(V.reciprocal(rstd[:, :], rstd[:, :]))
                chain.all()

            def normalise(src, k):
                part = src[:, GC * k:GC * k + GC, :]
                V.tensor_tensor(part, part, rstd[:, :].unsqueeze(1).broadcast_to((P, GC, N)),
                                ALU.mult).then_inc(normed, 1)

            for k in range(4):
                dve.nop(nofuse=True).then_inc(src_ready, 1)
            weights_ahead(0)
            split_low(1, ybT)

            def gate_b(i):
                c = C_OUT + i
                ready(c)
                g_ = sgB[:, bass.ds(i * GC, GC), :]
                V.tensor_tensor(g_, group(c), g_, ALU.mult).then_inc(psum_free, 1)

            def first_normalised():
                invert(0)
                normalise(cyT, 0)

            product(0, gate_b, {(0, 6): lambda: centre(cyT, 0, 0), (0, 7): lambda: centre(cyT, 0, 1),
                                (1, 0): lambda: centre(cyT, 0, 2), (1, 1): lambda: centre(cyT, 0, 3),
                                (3, 0): lambda: variance(0, 4), (3, 1): first_normalised,
                                (3, 2): lambda: normalise(cyT, 1), (3, 4): lambda: normalise(cyT, 2),
                                (3, 5): lambda: normalise(cyT, 3)})
            weights_ahead(1)
            split_low_part(2, 0, cyT)
            gate_b(NG - 1)
            for k in range(1, 4):
                split_low_part(2, k, cyT)

            def gate_a(i):
                c = C_OUT + NG + i
                ready(c)
                g_ = sgA[:, bass.ds(i * GC, GC), :]
                chain.link(V.tensor_tensor(g_, group(c), g_, ALU.mult))
                chain.all()
                V.tensor_tensor(g_, g_, sgB[:, bass.ds(i * GC, GC), :], ALU.add).then_inc(psum_free, 1)

            product(1, gate_a)
            weights_ahead(2)
            split_low_part(3, 0, sgA)
            gate_a(NG - 1)
            dve.wait_ge(psum_free, C_OUT + 2 * NG)
            dve.nop(nofuse=True).then_inc(gates_done, 1)
            for k in range(1, 4):
                split_low_part(3, k, sgA)

            def residual(i):
                c = C_OUT + 2 * NG + i
                ready(c)
                by = modT[:, bass.ds(G1 * NCH + i * GC, GC), :]
                chain.link(V.tensor_tensor(sampleM[:, :, :, :],
                                           ps[:, bass.ds(bank_set(c), 4), SEQ:N].rearrange("p n (b t) -> p n b t", b=DEC_B),
                                           by[:, :, 1:NMC].unsqueeze(3).broadcast_to((P, GC, DEC_B, DEC_T)), ALU.mult))
                for n in range(GC):
                    xs_ = xT[:, bass.ds(i * GC + n, 1), 0:SEQ].rearrange("p a t -> p (a t)")
                    src = ps[:, bass.ds(bank_set(c) + n, 1), 0:SEQ].rearrange("p a t -> p (a t)")
                    sc_ = modT[:, bass.ds(G1 * NCH + i * GC + n, 1), 0:1].rearrange("p a t -> p (a t)")
                    chain.link(V.scalar_tensor_tensor(out=xs_, in0=src, scalar=sc_, in1=xs_,
                                                      op0=ALU.mult, op1=ALU.add))
                chain.all()
                xs_ = xT[:, bass.ds(i * GC, GC), SEQ:N]
                V.tensor_tensor(xs_, xs_, sampleM[:, :, :, :].rearrange("p n b t -> p n (b t)"), ALU.add)\
                 .then_inc(psum_free, 1)

            def u2_factors():
                sc_ = modT[:, SC2 * NCH:(SC2 + 1) * NCH, :]
                sh_ = modT[:, SH2 * NCH:(SH2 + 1) * NCH, :]
                chain.link(V.tensor_tensor(modB[:, :, :], par[:, :, R_1B:R_1B + 1].broadcast_to((P, NCH, NMC)),
                                           sc_, ALU.mult))
                chain.all()
                chain.link(V.tensor_tensor(sh_, sh_, modB[:, :, :], ALU.add))
                chain.link(V.tensor_tensor(sc_, sc_, par[:, :, R_1G:R_1G + 1].broadcast_to((P, NCH, NMC)), ALU.mult))
                chain.all()

            product(2, residual, {(0, 5): u2_factors})
            weights_ahead(3)
            residual(NG - 1)
            dve.wait_ge(psum_free, C_OUT + 3 * NG)
            for k in range(4):
                centre(xT, 1, k)
            variance(1, 1)
            invert(1)

            def u2_samples(k):
                dve.wait_ge(normed, 4 + k + 1)
                part = slice(GC * k, GC * k + GC)
                by = modT[:, SC2 * NCH + GC * k:SC2 * NCH + GC * k + GC, 1:NMC]
                off = modT[:, SH2 * NCH + GC * k:SH2 * NCH + GC * k + GC, 1:NMC]
                out = tokens4(ybT[:, part, SEQ:N])
                chain.link(V.tensor_tensor(out, tokens4(xT[:, part, SEQ:N]),
                                           by.unsqueeze(3).broadcast_to((P, GC, DEC_B, DEC_T)), ALU.mult))
                chain.all()
                V.tensor_tensor(out, out, off.unsqueeze(3).broadcast_to((P, GC, DEC_B, DEC_T)), ALU.add)\
                 .then_inc(src_ready, 1)

            for k in range(4):
                normalise(xT, k)
                u2_samples(k)
                if k > 0:
                    split_low_part(4, k - 1, ybT)
            split_low_part(4, 3, ybT)

            def top16(vals, src, spare, index):
                jobs = list(zip(vals, src, spare, index))
                for v, a, b, x in jobs:
                    chain.link(V.max(v[:, 0:8], a))
                for v, a, b, x in jobs:
                    chain.back(len(jobs) - 1)
                    chain.link(V.max_index(x[:, 0:8], v[:, 0:8], a))
                    chain.link(V.match_replace(b, v[:, 0:8], a, LOWEST))
                chain.all()
                for v, a, b, x in jobs:
                    chain.link(V.max(v[:, 8:16], b))
                chain.all()
                for v, a, b, x in jobs:
                    chain.link(V.max_index(x[:, 8:16], v[:, 8:16], b))
                chain.all()

            def take_scores(s):
                chain.link(V.tensor_copy(sc0[:, :, :], scores[:, bass.ds(s, 1), :, :].rearrange("p a s k -> p (a s) k")))
                chain.all()

            def candidates():
                top16([top[:, 0, :], top[:, 1, :]], [sc0[:, 0, :], sc0[:, 1, :]],
                      [sc1[:, 0, :], sc1[:, 1, :]], [topIx[:, 0, :], topIx[:, 1, :]])
                chain.link(V.tensor_scalar(topIxF[:, 0, :], topIx[:, 0, :], float(NKEYS), None, ALU.mult))
                chain.link(V.tensor_copy(topIxF[:, 1, :], topIx[:, 1, :]))
                chain.all()
                for out, src in ((cand, top), (candId, topIxF)):
                    o = 0
                    for i, r, n in BLOCKS:
                        chain.link(V.tensor_tensor(
                            out[:, o:o + r * n].rearrange("p (r n) -> p r n", r=r),
                            src[:, 0, i:i + r].unsqueeze(2).broadcast_to((P, r, n)),
                            src[:, 1, 0:n].unsqueeze(1).broadcast_to((P, r, n)), ALU.add))
                        o += r * n
                chain.all()

            def choose(par_):
                top16([best[:, par_, :]], [cand[:, :]], [cand2[:, :]], [pos[:, :]])
                chain.link(V.tensor_copy(posF[:, :], pos[:, :]))
                chain.link(V.tensor_scalar(negMax[:, par_:par_ + 1], best[:, par_, 0:1], -1.0, None, ALU.mult))
                chain.all()
                chain.link(V.tensor_tensor(onehot[:, :, :], iotaF[:, :].unsqueeze(1).broadcast_to((P, TOPK, NCAND)),
                                           posF[:, :].unsqueeze(2).broadcast_to((P, TOPK, NCAND)), ALU.is_equal))
                chain.all()
                chain.link(V.tensor_tensor(onehot[:, :, :], onehot[:, :, :],
                                           candId[:, :].unsqueeze(1).broadcast_to((P, TOPK, NCAND)), ALU.mult))
                chain.all()
                chain.link(V.reduce_sum(eidF[:, :], onehot[:, :, :], AX.X))
                chain.all()
                V.tensor_copy(idxU[:, par_, :], eidF[:, :]).then_inc(idx_ready, 1)

            def route(s, par_):
                take_scores(s)
                candidates()
                choose(par_)

            def constants():
                dve.wait_ge(const_ready, 6)
                chain.link(V.tensor_copy(iotaF[:, :], iota[:, :]))
                chain.link(V.tensor_tensor(fold[:, :], ident[:, 0:TS], ident[:, TS:2 * TS], ALU.add))
                for r in range(2, 4):
                    chain.all()
                    chain.link(V.tensor_tensor(fold[:, :], fold[:, :], ident[:, TS * r:TS * r + TS], ALU.add))
                chain.all()

            def first_candidates():
                dve.wait_ge(scores_out, 1)
                candidates()

            def first_choice():
                choose(0)
                dve.wait_ge(idx_ready, 1)
                V.tensor_copy(idxV[:, 0, :], idxU[:, 0, :]).then_inc(idxv_ready, 1)

            hooks = {(1, 0): constants, (2, 1): first_candidates, (2, 3): first_choice}
            for i in range(NG):
                for u in range(AHEAD if i == 0 else 0, UNITS):
                    weights(C_OUT + 3 * NG + i, u)
                    if (i, u) in hooks:
                        hooks[i, u]()

            def step(s, par_, more=True, first=False, pieces=()):
                chain.restart()
                if more and not first:
                    route(s + 1, 1 - par_)
                for k in range(TOPK):
                    at_least_apart(dve, u_in[k % 4], 16 * (4 * s + k // 4 + 1))
                    row = uRing[k % 4][:, :]
                    V.scalar_tensor_tensor(out=row, in0=row, scalar=1.0, in1=ps[:, 0:4, :].rearrange("p b n -> p (b n)"),
                                           op0=ALU.mult, op1=ALU.mult,
                                           accum_out=dots[:, par_, k:k + 1]).then_inc(dot_done, 1)
                    if k == 0 and not first:
                        V.tensor_copy(idxV[:, par_, :], idxU[:, par_, :]).then_inc(idxv_ready, 1)
                    if k < len(pieces):
                        pieces[k]()
                    if first and k == TOPK // 2:
                        dve.wait_ge(scores_out, 2)
                        route(s + 1, 1 - par_)
                at_least_apart(dve, act_done, 2 * (s + 1))
                chain.link(V.reciprocal(exInv[:, :], exSum[:, :]))
                chain.link(V.tensor_tensor(ex[:, :], ex[:, :], gel[:, :], ALU.mult))
                chain.all()
                V.tensor_scalar(wts[:, par_, :], ex[:, :], exInv[:, :], None, ALU.mult).then_inc(wts_ready, 1)
                at_least_apart(dve, wts_ready, s + 1)
                at_least_apart(dve, idxv_ready, s + 1)

            def take_sum(t):
                m = ROWS[t]
                dve.wait_ge(v_done, TOPK * (TILES[t][1] + 1))
                at_least(dve, y_out, 16 * t)
                if t == SAMPLES:
                    V.tensor_copy(fin[:, :], ps[:, 4:8, :].rearrange("p b n -> p (b n)")).then_inc(fs_ready, 1)
                    dve.wait_ge(folded, 1)
                V.tensor_tensor(fin[0:m, :], ps[0:m, 4:8, :].rearrange("p b n -> p (b n)"),
                                (g2S if t == SAMPLES else g2P)[0:m, :], ALU.mult).then_inc(f_free, 1)
                dve.wait_ge(f_free, t + 1)

            def finish(t):
                m = ROWS[t]
                f = fin[0:m, :]

                def residual2():
                    chain.link(V.tensor_tensor(f, f, x1Tok[t][0:m, :], ALU.add))
                    chain.all()

                def statistics():
                    for n in range(4):
                        chain.link(V.bn_stats(stats[0:m, n, :], fin[0:m, n * 512:(n + 1) * 512]))
                    chain.all()

                def moments():
                    chain.link(V.bn_aggr(mv[0:m, :], stats[0:m, :, :].rearrange("p a b -> p (a b)")))
                    chain.all()
                    V.tensor_scalar(ve[0:m, 0:1], mv[0:m, 1:2], EPS, None, ALU.add).then_inc(ve_ready, 1)

                def centre2():
                    chain.link(V.scalar_tensor_tensor(out=f, in0=f, scalar=mv[0:m, 0:1], in1=lnG[0:m, :],
                                                      op0=ALU.subtract, op1=ALU.mult))
                    dve.wait_ge(sdev_ready, t + 1)
                    chain.link(V.reciprocal(ve[0:m, 2:3], ve[0:m, 1:2]))
                    chain.all()

                def normalise2():
                    V.scalar_tensor_tensor(out=f, in0=f, scalar=ve[0:m, 2:3], in1=lnB[0:m, :],
                                           op0=ALU.mult, op1=ALU.add).then_inc(y_ready, 1)

                return [residual2, statistics, moments, centre2, normalise2]

            for t, (a, b) in enumerate(TILES):
                dve.wait_ge(u2_ready, t + 1)
                step(a, 0, first=(t == 0))
                if t == 0:
                    dve.wait_ge(scores_out, 1 + len(SCORE_ROUNDS))
                    dve.wait_ge(ln_in, 32)
                else:
                    take_sum(t - 1)
                step(a + 1, 1, pieces=finish(t - 1) if t > 0 else ())
                chain.restart()
                if t < 2 and b - a > 1:
                    with dve.Fori(0, (b - a - 1) // 2) as i:
                        step(a + 2 + 2 * i, 0)
                        step(a + 3 + 2 * i, 1)
                if t == 2:
                    with dve.Fori(0, (b - a - 3) // 2) as i:
                        step(a + 2 + 2 * i, 0)
                        step(a + 3 + 2 * i, 1)
                    step(b - 1, 0)
                    step(b, 1, more=False)
            chain.restart()
            take_sum(2)
            for piece in finish(2):
                piece()
            dve.wait_ge(y_ready, 3)


def kernel(**inputs):
    import numpy as np
    import concourse.bacc as bacc
    from concourse.bass_utils import run_bass_kernel_spmd

    rows = lambda a: a.reshape(-1, a.shape[-1])
    b_mod = np.asarray(inputs["b_mod"])
    arrays = {
        "x_prompt": rows(np.asarray(inputs["x_prompt"])), "x_sample": rows(np.asarray(inputs["x_sample"])),
        "state_a": rows(np.asarray(inputs["state_conv_a"])), "state_b": rows(np.asarray(inputs["state_conv_b"])),
        "c_prompt": np.asarray(inputs["c_prompt"]), "c_sample": np.asarray(inputs["c_sample"]),
        "w_mod": np.asarray(inputs["w_mod"])[0], "b_mod": b_mod.reshape(6, -1),
        "w_in": np.asarray(inputs["w_in"])[0], "conv_a_w": np.asarray(inputs["conv_a_w"])[0],
        "conv_a_b": np.asarray(inputs["conv_a_b"]), "ln_a_g": np.asarray(inputs["ln_a_g"]),
        "ln_a_b": np.asarray(inputs["ln_a_b"]), "w_a_out": np.asarray(inputs["w_a_out"])[0],
        "conv_b_w": np.asarray(inputs["conv_b_w"])[0], "w_b_out": np.asarray(inputs["w_b_out"])[0],
        "w_o": np.asarray(inputs["w_o"])[0], "ln1_g": np.asarray(inputs["ln1_g"]),
        "ln1_b": np.asarray(inputs["ln1_b"]), "w_q": np.asarray(inputs["w_q"])[0],
        "sub_keys": np.asarray(inputs["sub_keys"])[0], "peer_u": np.asarray(inputs["peer_u"])[0],
        "peer_v": np.asarray(inputs["peer_v"])[0], "ln2_g": np.asarray(inputs["ln2_g"]),
        "ln2_b": np.asarray(inputs["ln2_b"]),
    }
    outs = [("y_prompt", (SEQ, D)), ("y_sample", (TS, D)), ("new_a_prompt", (HA, D)), ("new_b_prompt", (HB, D)),
            ("new_a_sample", (DEC_B, HA, D)), ("new_b_sample", (DEC_B, HB, D))]
    nc = bacc.Bacc("TRN2", target_bir_lowering=False, num_devices=1)
    aps, feed = [], {}
    for name, a in arrays.items():
        a = np.ascontiguousarray(a)
        feed[f"in_{name}"] = a
        aps.append(nc.dram_tensor(f"in_{name}", a.shape, mybir.dt.from_np(a.dtype), kind="ExternalInput").ap())
    for name, shape in outs:
        aps.append(nc.dram_tensor(f"out_{name}", shape, F32, kind="ExternalOutput").ap())
    hybrid_step(nc, *aps)
    r = run_bass_kernel_spmd(nc, [feed], core_ids=[0]).results[0]
    y_p, y_s, a_p, b_p, a_s, b_s = (r[f"out_{name}"] for name, _ in outs)
    return (y_p.reshape(1, SEQ, D), y_s.reshape(DEC_B, DEC_T, D), a_p.reshape(1, 1, HA, D),
            b_p.reshape(1, 1, HB, D), a_s.reshape(1, DEC_B, HA, D), b_s.reshape(1, DEC_B, HB, D))
```
